# Optimizing a Trainium2 kernel written in Bass

```python
import jax, jax.numpy as jnp
from jax import lax
import numpy as np

D_MODEL = 1024
BATCH = 1
SEQ = 256
DEPTH = 2

EPS = 1e-6
ROPE_THETA = 10000.0
N_BRANCH = 3
LRU_WIDTH = 512
LRU_BLOCKS = 8
LRU_BLOCK = LRU_WIDTH // LRU_BLOCKS
LRU_CONV = 4
LRU_C = 8.0
RET_HEADS = 8
RET_DK = 64
RET_DV = 64
RET_CHUNK = 128
MLA_HEADS = 8
MLA_Q_RANK = 384
MLA_KV_RANK = 256
MLA_NOPE = 64
MLA_ROPE = 32
MLA_V = 64
ATTN_BLOCK = 128
D_FF = 2816
FFN_CONV = 3

IN_SIZES = (LRU_WIDTH, LRU_WIDTH,
            RET_HEADS * RET_DK, RET_HEADS * RET_DK, RET_HEADS * RET_DV, RET_HEADS * RET_DV,
            MLA_Q_RANK, MLA_KV_RANK, MLA_ROPE,
            N_BRANCH * D_MODEL)
N_IN = (2 * LRU_WIDTH + 2 * RET_HEADS * RET_DK + 2 * RET_HEADS * RET_DV
        + MLA_Q_RANK + MLA_KV_RANK + MLA_ROPE + N_BRANCH * D_MODEL)

kernel_name = "hybrid_lru_retention_mla_convglu"

def rmsnorm(x, g):
    xf = x.astype(jnp.float32)
    y = xf * lax.rsqrt(jnp.mean(xf * xf, axis=-1, keepdims=True) + EPS)
    return (y * g.astype(jnp.float32)).astype(x.dtype)

def modulate(h, shift, scale):
    return h * (1.0 + scale[:, None, :]) + shift[:, None, :]

def causal_dwconv(x, w, b):
    k_w = w.shape[0]
    s = x.shape[1]
    xp = jnp.pad(x, ((0, 0), (k_w - 1, 0), (0, 0)))
    y = xp[:, k_w - 1:k_w - 1 + s] * w[k_w - 1] + b
    for k in range(k_w - 1):
        y = y + xp[:, k:k + s] * w[k]
    return y

def rope_tables(positions, dim):
    inv = ROPE_THETA ** (-jnp.arange(0, dim, 2, dtype=jnp.float32) / dim)
    ang = positions.astype(jnp.float32)[..., None] * inv
    return jnp.cos(ang), jnp.sin(ang)

def apply_rope(x, cos, sin):
    half = x.shape[-1] // 2
    x1, x2 = x[..., :half], x[..., half:]
    y = jnp.concatenate([x1 * cos - x2 * sin, x1 * sin + x2 * cos], axis=-1)
    return y.astype(x.dtype)

def split_cols(t):
    out = []
    start = 0
    for n in IN_SIZES:
        out.append(t[..., start:start + n])
        start += n
    return out

def rglru_branch(xb, gb, conv_w, conv_b, wa, ba, wx, bx, lam):
    bsz, s, _ = xb.shape
    xc = causal_dwconv(xb, conv_w, conv_b)
    xblk = xc.reshape(bsz, s, LRU_BLOCKS, LRU_BLOCK)
    r = jax.nn.sigmoid(jnp.einsum('bsnh,nhk->bsnk', xblk, wa).reshape(bsz, s, LRU_WIDTH) + ba)
    i = jax.nn.sigmoid(jnp.einsum('bsnh,nhk->bsnk', xblk, wx).reshape(bsz, s, LRU_WIDTH) + bx)
    log_a = -LRU_C * r.astype(jnp.float32) * jax.nn.softplus(-lam.astype(jnp.float32))
    a = jnp.exp(log_a)
    mult = jnp.sqrt(-jnp.expm1(2.0 * log_a))
    u = mult * (i * xc).astype(jnp.float32)

    def combine(p, q):
        a1, b1 = p
        a2, b2 = q
        return a1 * a2, a2 * b1 + b2

    _, h = lax.associative_scan(combine, (a, u), axis=1)
    return h.astype(xb.dtype) * jax.nn.gelu(gb)

def retention_branch(q, k, v, g, cos, sin):
    bsz, s, _ = q.shape
    nc = s // RET_CHUNK
    f32 = jnp.float32
    q = apply_rope(q.reshape(bsz, s, RET_HEADS, RET_DK), cos[:, :, None, :], sin[:, :, None, :]).astype(f32)
    k = apply_rope(k.reshape(bsz, s, RET_HEADS, RET_DK), cos[:, :, None, :], sin[:, :, None, :]).astype(f32)
    k = k * (RET_DK ** -0.5)
    v = v.reshape(bsz, s, RET_HEADS, RET_DV).astype(f32)

    log_gamma = jnp.log1p(-(2.0 ** (-5.0 - jnp.arange(RET_HEADS, dtype=f32))))
    idx = jnp.arange(RET_CHUNK, dtype=f32)
    diff = idx[:, None] - idx[None, :]
    causal = diff >= 0
    inner_decay = jnp.where(causal[None], jnp.exp(jnp.where(causal, diff, 0.0)[None] * log_gamma[:, None, None]), 0.0)
    kv_decay = jnp.exp((RET_CHUNK - 1.0 - idx)[None, :] * log_gamma[:, None])
    q_decay = jnp.exp((idx + 1.0)[:, None] * log_gamma[None, :])
    chunk_decay = jnp.exp(RET_CHUNK * log_gamma)

    qc = q.reshape(bsz, nc, RET_CHUNK, RET_HEADS, RET_DK)
    kc = k.reshape(bsz, nc, RET_CHUNK, RET_HEADS, RET_DK)
    vc = v.reshape(bsz, nc, RET_CHUNK, RET_HEADS, RET_DV)

    scores = jnp.einsum('bnchd,bnshd->bnhcs', qc, kc) * inner_decay
    y_inner = jnp.einsum('bnhcs,bnshe->bnche', scores, vc)

    kv = jnp.einsum('bnshd,bnshe,hs->nbhde', kc, vc, kv_decay)

    def step(state, kv_n):
        return state * chunk_decay[None, :, None, None] + kv_n, state

    _, s_prev = lax.scan(step, jnp.zeros((bsz, RET_HEADS, RET_DK, RET_DV), f32), kv)
    y_cross = jnp.einsum('bnchd,nbhde->bnche', qc, s_prev) * q_decay[None, None, :, :, None]

    y = (y_inner + y_cross).reshape(bsz, s, RET_HEADS, RET_DV)
    mu = jnp.mean(y, axis=-1, keepdims=True)
    var = jnp.mean(jnp.square(y - mu), axis=-1, keepdims=True)
    y = ((y - mu) * lax.rsqrt(var + EPS)).reshape(bsz, s, RET_HEADS * RET_DV).astype(g.dtype)
    return jax.nn.silu(g) * y

def mla_branch(cq, ckv, kr, q_norm_g, w_uq, kv_norm_g, w_ukv, cos, sin):
    bsz, s, _ = cq.shape
    dqk = MLA_NOPE + MLA_ROPE
    q = (rmsnorm(cq, q_norm_g) @ w_uq).reshape(bsz, s, MLA_HEADS, dqk)
    q_nope, q_rope = q[..., :MLA_NOPE], q[..., MLA_NOPE:]
    q_rope = apply_rope(q_rope, cos[:, :, None, :], sin[:, :, None, :])
    kvu = (rmsnorm(ckv, kv_norm_g) @ w_ukv).reshape(bsz, s, MLA_HEADS, MLA_NOPE + MLA_V)
    k_nope, v = kvu[..., :MLA_NOPE], kvu[..., MLA_NOPE:]
    k_rope = apply_rope(kr, cos, sin)
    q = jnp.concatenate([q_nope, q_rope], axis=-1)
    k = jnp.concatenate([k_nope, jnp.broadcast_to(k_rope[:, :, None, :], (bsz, s, MLA_HEADS, MLA_ROPE))], axis=-1)
    scale = dqk ** -0.5
    nb = s // ATTN_BLOCK
    qb = q.reshape(bsz, nb, ATTN_BLOCK, MLA_HEADS, dqk).transpose(1, 0, 2, 3, 4)
    key_idx = jnp.arange(s)

    def attend(args):
        q_blk, start = args
        sc = jnp.einsum('bqhd,bkhd->bhqk', q_blk, k).astype(jnp.float32) * scale
        q_idx = start + jnp.arange(ATTN_BLOCK)
        mask = key_idx[None, :] <= q_idx[:, None]
        sc = jnp.where(mask[None, None], sc, -1e30)
        p = jax.nn.softmax(sc, axis=-1).astype(v.dtype)
        return jnp.einsum('bhqk,bkhe->bqhe', p, v)

    o = lax.map(attend, (qb, jnp.arange(nb) * ATTN_BLOCK))
    return o.transpose(1, 0, 2, 3, 4).reshape(bsz, s, MLA_HEADS * MLA_V)

def mixer_sublayer(h, w_in, lru_conv_w, lru_conv_b, lru_wa, lru_ba, lru_wx, lru_bx, lru_lambda, lru_wo,
                   ret_wo, mla_q_norm_g, mla_w_uq, mla_kv_norm_g, mla_w_ukv, mla_wo, w_out,
                   cos_r, sin_r, cos_m, sin_m):
    bsz, s, _ = h.shape
    t = h @ w_in
    lru_x, lru_g, ret_q, ret_k, ret_v, ret_g, mla_cq, mla_ckv, mla_kr, gate_logits = split_cols(t)
    y_lru = rglru_branch(lru_x, lru_g, lru_conv_w, lru_conv_b, lru_wa, lru_ba, lru_wx, lru_bx, lru_lambda) @ lru_wo
    y_ret = retention_branch(ret_q, ret_k, ret_v, ret_g, cos_r, sin_r) @ ret_wo
    y_mla = mla_branch(mla_cq, mla_ckv, mla_kr, mla_q_norm_g, mla_w_uq, mla_kv_norm_g, mla_w_ukv, cos_m, sin_m) @ mla_wo
    gates = jax.nn.sigmoid(gate_logits).reshape(bsz, s, N_BRANCH, D_MODEL)
    merged = gates[:, :, 0] * y_lru + gates[:, :, 1] * y_ret + gates[:, :, 2] * y_mla
    return merged @ w_out

def conv_glu(h, w_up, conv_w, conv_b, w_down):
    up = causal_dwconv(h @ w_up, conv_w, conv_b)
    u, g = up[..., :D_FF], up[..., D_FF:]
    return (jax.nn.gelu(g) * u) @ w_down

def setup_inputs(seed: int = 0) -> dict:
    key = jax.random.key(seed)
    ks = jax.random.split(key, 32)
    f32 = jnp.float32
    L = DEPTH

    def dense(k, shape, fan_in, gain=1.0):
        return jax.random.normal(k, shape, f32) * (gain * fan_in ** -0.5)

    def gain(k, shape):
        return 1.0 + 0.05 * jax.random.normal(k, shape, f32)

    def bias(k, shape):
        return 0.02 * jax.random.normal(k, shape, f32)

    offs = jax.random.randint(ks[2], (BATCH, 1), 0, 4096, dtype=jnp.int32)
    positions = (offs + jnp.arange(SEQ, dtype=jnp.int32)[None, :]).astype(jnp.int32)
    a_c = jax.random.uniform(ks[12], (L, LRU_WIDTH), f32, minval=0.9, maxval=0.999)
    a_base = a_c ** (1.0 / LRU_C)
    lru_lambda = jnp.log(a_base) - jnp.log1p(-a_base)
    return {
        "x": jax.random.normal(ks[0], (BATCH, SEQ, D_MODEL), f32),
        "c": jax.random.normal(ks[1], (BATCH, D_MODEL), f32),
        "positions": positions,
        "ada_w": dense(ks[3], (L, D_MODEL, 6 * D_MODEL), D_MODEL, 0.5),
        "ada_b": bias(ks[4], (L, 6 * D_MODEL)),
        "mix_pre_g": gain(ks[5], (L, D_MODEL)),
        "mix_post_g": gain(ks[6], (L, D_MODEL)),
        "w_in": dense(ks[7], (L, D_MODEL, N_IN), D_MODEL),
        "lru_conv_w": dense(ks[8], (L, LRU_CONV, LRU_WIDTH), LRU_CONV),
        "lru_conv_b": bias(ks[9], (L, LRU_WIDTH)),
        "lru_wa": dense(ks[10], (L, LRU_BLOCKS, LRU_BLOCK, LRU_BLOCK), LRU_BLOCK),
        "lru_ba": bias(ks[11], (L, LRU_WIDTH)),
        "lru_wx": dense(ks[13], (L, LRU_BLOCKS, LRU_BLOCK, LRU_BLOCK), LRU_BLOCK),
        "lru_bx": bias(ks[14], (L, LRU_WIDTH)),
        "lru_lambda": lru_lambda,
        "lru_wo": dense(ks[15], (L, LRU_WIDTH, D_MODEL), LRU_WIDTH),
        "ret_wo": dense(ks[16], (L, RET_HEADS * RET_DV, D_MODEL), RET_HEADS * RET_DV),
        "mla_q_norm_g": gain(ks[17], (L, MLA_Q_RANK)),
        "mla_w_uq": dense(ks[18], (L, MLA_Q_RANK, MLA_HEADS * (MLA_NOPE + MLA_ROPE)), MLA_Q_RANK),
        "mla_kv_norm_g": gain(ks[19], (L, MLA_KV_RANK)),
        "mla_w_ukv": dense(ks[20], (L, MLA_KV_RANK, MLA_HEADS * (MLA_NOPE + MLA_V)), MLA_KV_RANK),
        "mla_wo": dense(ks[21], (L, MLA_HEADS * MLA_V, D_MODEL), MLA_HEADS * MLA_V),
        "w_out": dense(ks[22], (L, D_MODEL, D_MODEL), D_MODEL),
        "ffn_pre_g": gain(ks[23], (L, D_MODEL)),
        "ffn_post_g": gain(ks[24], (L, D_MODEL)),
        "ffn_w_up": dense(ks[25], (L, D_MODEL, 2 * D_FF), D_MODEL),
        "ffn_conv_w": dense(ks[26], (L, FFN_CONV, 2 * D_FF), FFN_CONV),
        "ffn_conv_b": bias(ks[27], (L, 2 * D_FF)),
        "ffn_w_down": dense(ks[28], (L, D_FF, D_MODEL), D_FF),
    }

def reference(x, c, positions, ada_w, ada_b, mix_pre_g, mix_post_g, w_in, lru_conv_w, lru_conv_b,
              lru_wa, lru_ba, lru_wx, lru_bx, lru_lambda, lru_wo, ret_wo, mla_q_norm_g, mla_w_uq,
              mla_kv_norm_g, mla_w_ukv, mla_wo, w_out, ffn_pre_g, ffn_post_g, ffn_w_up, ffn_conv_w,
              ffn_conv_b, ffn_w_down):
    cos_r, sin_r = rope_tables(positions, RET_DK)
    cos_m, sin_m = rope_tables(positions, MLA_ROPE)
    c_act = jax.nn.silu(c)
    for l in range(DEPTH):
        mod = c_act @ ada_w[l] + ada_b[l]
        sh_m, sc_m, g_m, sh_f, sc_f, g_f = jnp.split(mod, 6, axis=-1)
        h = modulate(rmsnorm(x, mix_pre_g[l]), sh_m, sc_m)
        y = mixer_sublayer(h, w_in[l], lru_conv_w[l], lru_conv_b[l], lru_wa[l], lru_ba[l], lru_wx[l],
                           lru_bx[l], lru_lambda[l], lru_wo[l], ret_wo[l], mla_q_norm_g[l], mla_w_uq[l],
                           mla_kv_norm_g[l], mla_w_ukv[l], mla_wo[l], w_out[l],
                           cos_r, sin_r, cos_m, sin_m)
        x = x + g_m[:, None, :] * rmsnorm(y, mix_post_g[l])
        h = modulate(rmsnorm(x, ffn_pre_g[l]), sh_f, sc_f)
        y = conv_glu(h, ffn_w_up[l], ffn_conv_w[l], ffn_conv_b[l], ffn_w_down[l])
        x = x + g_f[:, None, :] * rmsnorm(y, ffn_post_g[l])
    return x


_drawn_inputs = setup_inputs


def setup_inputs(seed=0):
    import zlib

    import numpy as np

    out = dict(_drawn_inputs(seed))
    spreads = {}
    factors = {'lru_conv_b': 76.712,
     'lru_ba': 200.0,
     'lru_bx': 200.0,
     'mla_q_norm_g': 8.0,
     'mla_kv_norm_g': 7.324,
     'ffn_post_g': 2.817,
     'ffn_conv_b': 5.142,
     'lru_wa': 31.56,
     'lru_lambda': 22.224,
     'lru_conv_w': 8.0,
     'lru_wx': 8.0,
     'lru_wo': 8.0}
    for name, (base, spread) in spreads.items():
        noise = np.random.default_rng([zlib.crc32(name.encode()), seed]).standard_normal(out[name].shape)
        drawn = base * np.exp(spread * noise) if base else spread * noise
        out[name] = __import__('jax').numpy.asarray(drawn.astype(out[name].dtype))
    for name, factor in factors.items():
        out[name] = (out[name] * factor).astype(out[name].dtype)
    return out
```

```python
from contextlib import ExitStack

import numpy as np

import concourse.bass as bass
from concourse import mybir

P = 128
F32 = mybir.dt.float32
F32R = mybir.dt.float32r
I32 = mybir.dt.int32
ACT = mybir.ActivationFunctionType
ALU = mybir.AluOpType
AX_X = mybir.AxisListType.X

EPS = 1e-6
ROPE_THETA = 10000.0
LRU_C = 8.0
RING = 3
HEADS = 8
TINY = 2.0 ** -115



class Sig:

    def __init__(self, sem, per_layer):
        self.s = sem
        self.n = per_layer

    def at(self, l, k):
        return l * self.n + k


def constants(seq):
    f = np.arange(P)
    ident = np.eye(P)
    same_head = (f[:, None] // 64 == f[None, :] // 64).astype(np.float64)
    center = ident - same_head / 64.0
    mean64 = same_head / 64.0
    ones = np.ones((P, P))

    def rotation(dim):
        half = dim // 2
        r = np.zeros((P, P))
        for m in range(P):
            if m % dim < half:
                r[m + half, m] = -1.0
            else:
                r[m - half, m] = 1.0
        return r

    t = np.arange(seq)[None, :]
    s = np.arange(P)[:, None]
    log_gamma = np.log1p(-(2.0 ** (-5.0 - np.arange(HEADS))))
    diff = t - s
    decay = [np.where(diff >= 0, np.exp(np.maximum(diff, 0) * g), 0.0) * 64 ** -0.5 for g in log_gamma]
    diag = np.where(np.arange(P)[None, :] <= np.arange(P)[:, None], 0.0, -1e30)
    mask = np.concatenate([diag, np.zeros((P, P)), diag], axis=1)
    inv_ret = (ROPE_THETA ** (-np.arange(0, 64, 2) / 64.0))[f % 32][:, None]
    inv_mla = (ROPE_THETA ** (-np.arange(0, 32, 2) / 32.0))[f % 16][:, None]
    eps = np.full((P, 1), EPS)
    parts = [ident, center, mean64, ones, rotation(64), rotation(32), *decay, mask, inv_ret, inv_mla, eps]
    return np.concatenate(parts, axis=1).astype(np.float32)


def trunk_kernel(nc, A, consts, out):
    L, D, N_ADA = A["ada_w"].shape
    T = A["x"].shape[1]
    DK = D // P
    TC = T // P
    FF = A["ffn_w_down"].shape[1]
    NFF = FF // P
    W = A["lru_wo"].shape[1]
    WK = W // P
    QR = A["mla_w_uq"].shape[1]
    KVR = A["mla_w_ukv"].shape[1]
    QK, KVK = QR // P, KVR // P
    DQK = A["mla_w_uq"].shape[2] // HEADS
    NCONST = consts.shape[1]
    assert (D, T, FF, W, QR, KVR, DQK) == (1024, 256, 2816, 512, 384, 256, 96)
    SCALE = DQK ** -0.5

    o_rq, o_rk, o_rv, o_rg = 2 * W, 3 * W, 4 * W, 5 * W
    o_cq = 6 * W
    o_gate = o_cq + QR + KVR + 32
    BW = 256

    def win(l, c0, cols):
        return A["w_in"][bass.ds(l, 1)].rearrange("a (k p) n -> p (a k) n", p=P)[:, :, c0:c0 + cols]

    def rows(name, l, k0, k1, c0, cols):
        return A[name][bass.ds(l, 1)].rearrange("a (k p) n -> p (a k) n", p=P)[:, k0:k1, c0:c0 + cols]

    mixer_blocks = []
    J = {}

    def block(name, src, k, cols):
        J[name] = len(mixer_blocks)
        mixer_blocks.append((src, k, cols))

    for i in range(2):
        block(("q", i), lambda l, i=i: win(l, o_rq + BW * i, BW), DK, BW)
    for i in range(2):
        block(("k", i), lambda l, i=i: win(l, o_rk + BW * i, BW), DK, BW)
    for i in range(2):
        block(("v", i), lambda l, i=i: rows("w_in", l, 4 * i, 4 * i + 4, o_rv, W), 4, W)
    for i in range(2):
        block(("g", i), lambda l, i=i: win(l, o_rg + BW * i, BW), DK, BW)
    for i in range(2):
        block(("lx", i), lambda l, i=i: win(l, BW * i, BW), DK, BW)
    for i in range(2):
        block(("lg", i), lambda l, i=i: win(l, W + BW * i, BW), DK, BW)
    block(("c", 0), lambda l: win(l, o_cq, BW), DK, BW)
    block(("c", 1), lambda l: win(l, o_cq + BW, BW), DK, BW)
    block(("c", 2), lambda l: win(l, o_cq + 2 * BW, P + 32), DK, P + 32)
    for i in range(2):
        block(("uq", i), lambda l, i=i: rows("mla_w_uq", l, 0, QK, 4 * DQK * i, 4 * DQK), QK, 4 * DQK)
    block(("ukv", 0), lambda l: rows("mla_w_ukv", l, 0, KVK, 0, D), KVK, D)
    for b, wo in enumerate(("ret_wo", "lru_wo", "mla_wo")):
        for i in range(4):
            block(("gate", b, i), lambda l, c=o_gate + D * (1, 0, 2)[b] + BW * i: win(l, c, BW), DK, BW)
            if i % 2 == 0:
                block(("wo", b, i // 2), lambda l, wo=wo, i=i: rows(wo, l, 0, WK, W * (i // 2), W), WK, W)
    for i in range(4):
        block(("out", i), lambda l, i=i: rows("w_out", l, 2 * i, 2 * i + 2, 0, D), 2, D)
    NM = len(mixer_blocks)
    PAIRS = NFF // 2
    NB = NM + 3 * PAIRS
    assert (NM, NB) == (40, 73)
    USES = [len(range(s, NB, RING)) for s in range(RING)]

    def previous(j):
        return j - RING if j >= RING else max(b for b in range(NB) if b % RING == j % RING) - NB

    ctx = ExitStack()
    with ctx:
        def sb(name, shape, dt=F32):
            return ctx.enter_context(nc.sbuf_tensor(name, shape, dt))

        def sem(name):
            return ctx.enter_context(nc.semaphore(name))

        def sig(name, per_layer):
            return Sig(sem(name), per_layer)

        PS = ctx.enter_context(nc.psum_tensor("banks", [P, 8, 512], F32))
        ADA_BANK = 7

        raw = sb("raw", [P, RING, 2048])
        w_hi = sb("w_hi", [P, RING, 2048], F32R)
        w_lo = sb("w_lo", [P, RING, 2048], F32R)
        x = sb("x", [P, TC, D])
        h32 = sb("h32", [P, DK, T])
        h_hi = sb("h_hi", [P, DK, T], F32R)
        h_lo = sb("h_lo", [P, DK, T], F32R)
        adw = sb("adw", [P, 2, 4, BW])
        adp = sb("adp", [P, 4, BW])
        adacc = sb("adacc", [P, 2, BW])
        grow = sb("grow", [P, D])
        cst = sb("cst", [P, NCONST])
        cosr, sinr = sb("cosr", [P, T]), sb("sinr", [P, T])
        cosm, sinm = sb("cosm", [P, T]), sb("sinm", [P, T])
        par = sb("par", [P, L, 3 * P])
        cur = sb("cur", [P, 3 * P])
        mod = sb("mod", [P, 24])
        hscale = sb("hscale", [P, DK])
        gcol = sb("gcol", [P, DK])
        cact = sb("cact", [P, DK])
        st = sb("st", [P, 16])
        mx = sb("mx", [P, 2, 8])
        spt = sb("spt", [P, 8, 2 * WK])
        AB = sb("AB", [P, 8, T])
        CD = sb("CD", [P, 8, T])
        EF = sb("EF", [P, 8, T])
        tmp = sb("tmp", [P, 5, T])
        lat = sb("lat", [P, 5, T])
        pbuf = sb("pbuf", [P, 2, 384])
        ptb = sb("ptb", [P, 2, 384])
        kr = sb("kr", [P, T])
        rs2 = pbuf[:, :, 0:T]
        oa_hi, oa_lo = sb("oa_hi", [P, 4, T], F32R), sb("oa_lo", [P, 4, T], F32R)
        ob_hi, ob_lo = sb("ob_hi", [P, 5, T], F32R), sb("ob_lo", [P, 5, T], F32R)
        wbd = sb("wbd", [P, 2, 4, P])
        pos_i = kr[:].bitcast(I32)

        def piece(i, n=P):
            return cst[:, i:i + n]

        ident, center, mean64, ones, rot_r, rot_m = (piece(P * i) for i in range(6))
        decay = cst[:, 6 * P:6 * P + HEADS * T].rearrange("p (h t) -> p h t", h=HEADS)
        c0 = 6 * P + HEADS * T
        mask = piece(c0, 3 * P)
        inv_ret, inv_mla, eps = (piece(c0 + 3 * P + i, 1) for i in range(3))

        col = {}
        layout = [
            [("tap0", 44), ("tap1", 44), ("mix_pre_g", 8), ("ffn_pre_g", 8), ("mix_post_g", 8), ("ffn_post_g", 8),
             ("mla_q_norm_g", 3), ("mla_kv_norm_g", 2)],
            [("tap2", 44), ("ffn_conv_b", 44), ("lru_conv_w", 16), ("lru_conv_b", 4), ("lru_ba", 4), ("lru_bx", 4),
             ("lru_lambda", 4)],
            [("ada_b", 48)],
        ]
        used = []
        for ch, vecs in enumerate(layout):
            n = 0
            for name, cnt in vecs:
                col[name] = ch * P + n
                n += cnt
            used.append(n)
        col["-8sp"], col["8sp"] = P + 120, P + 124

        def pc(name, i=0, n=1):
            return cur[:, col[name] + i:col[name] + i + n]

        raw_in = [sig(f"raw_in{s}", 16 * USES[s]) for s in range(RING)]
        hi_ready = sig("hi_ready", NB)
        lo_ready = sig("lo_ready", NB)
        blk_used = sig("blk_used", NB)
        c_in, cst_in, pos_in, x_in, rows_in = (sem(n) for n in ("c_in", "cst_in", "pos_in", "x_in", "rows_in"))
        ada_in = [sem(f"ada_in{i}") for i in range(2)]
        sig_c, cact_ready, pro = sem("sig_c"), sem("cact_ready"), sem("pro_dve")
        ada0_done = sem("ada0_done")
        ang_ready, trig_ready = sem("ang_ready"), sem("trig_ready")
        par_zero, par_ps, par_ready = sem("par_zero"), sem("par_ps"), sem("par_ready")
        sp_a, sp_d = sem("sp_act"), sem("sp_dve")
        adw_in = [sem(f"adw_in{i}") for i in range(2)]
        ad_op = sem("ad_op")
        acc_ready = sem("acc_ready")
        ada_sum = sem("ada_sum")
        ada0_sum = sem("ada0_sum")
        tick, sp_tick = sem("pool_tick"), sem("sp_tick")
        cur_ready = sig("cur_ready", 1)
        mod_evac, mod_ready = sig("mod_evac", 2), sig("mod_ready", 4)
        x_ready = sig("x_ready", 4)
        n_ss, n_sq, n_rs, n_xn = (sig(n, 4) for n in ("n_ss", "n_sq", "n_rs", "n_xn"))
        n_tp, n_ha, n_hd, n_hi, n_lo = sig("n_tp", 8), sig("n_ha", 4), sig("n_hd", 4), sig("n_hi", 4), sig("n_lo", 4)
        grow_ps, grow_ev = sig("grow_ps", 4), sig("grow_ev", 4)
        y_ps = sig("y_ps", 2)
        p_ss, p_sq, p_rs, p_y = (sig(n, 4) for n in ("p_ss", "p_sq", "p_rs", "p_y"))
        wbd_in, wbd_zero = sig("wbd_in", 256), sig("wbd_zero", 1)
        qk_ev, v_ev = sig("qk_ev", 4), sig("v_ev", 2)
        g_th, g_ev = sig("g_th", 2), sig("g_ev", 2)
        rot_ps, rot_t, rot_c, rope = sig("rot_ps", 4), sig("rot_t", 4), sig("rot_c", 4), sig("rope", 4)
        rs_ps, rs_p, rs_av = sig("rs_ps", 8), sig("rs_p", 8), sig("rs_av", 8)
        ry_ev, ry_ps = sig("ry_ev", 2), sig("ry_ps", 2)
        rv_sq, rv_ps, rv_sd, rv_rc = sig("rv_sq", 2), sig("rv_ps", 2), sig("rv_sd", 2), sig("rv_rc", 2)
        r_yn, r_o, r_ohi, r_olo = sig("r_yn", 2), sig("r_o", 2), sig("r_ohi", 2), sig("r_olo", 2)
        lx_c0, lx_c, lg_ev = sig("lx_c0", 2), sig("lx_c", 12), sig("lg_ev", 2)
        lr_ps, lr_ev = sig("lr_ps", 4), sig("lr_ev", 2)
        l_at, l_den, l_rcp, l_v = sig("l_at", 2), sig("l_den", 1), sig("l_rcp", 1), sig("l_v", 2)
        l_mult, l_ix, l_u, l_h, l_o = sig("l_mult", 1), sig("l_ix", 1), sig("l_u", 1), sig("l_h", 4), sig("l_o", 1)
        l_ohi, l_olo = sig("l_ohi", 1), sig("l_olo", 1)
        c_ev, kr_ev, c_sq = sig("c_ev", 1), sig("kr_ev", 1), sig("c_sq", 1)
        cs_ps, cs_sd, cs_rc = sig("cs_ps", 1), sig("cs_sd", 1), sig("cs_rc", 1)
        cn, cn_hi, cn_lo = sig("cn", 2), sig("cn_hi", 1), sig("cn_lo", 1)
        uq_ps, uq_ev = sig("uq_ps", 2), sig("uq_ev", 4)
        uk_ps, uk_ev = sig("uk_ps", 2), sig("uk_ev", 2)
        uv_ps, uv_ev = sig("uv_ps", 1), sig("uv_ev", 2)
        kt_ps, kt_t, kt_c, kt = sig("kt_ps", 1), sig("kt_t", 1), sig("kt_c", 1), sig("kt", 2)
        qt_ps, qt_t, qt_c, qt = sig("qt_ps", 4), sig("qt_t", 4), sig("qt_c", 4), sig("qt", 4)
        s_ps, s_m, s_max, s_neg = sig("s_ps", 8), sig("s_m", 8), sig("s_max", 8), sig("s_neg", 8)
        s_e, s_rc, s_n, s_tp, s_tev, s_av = (sig(n, 8) for n in ("s_e", "s_rc", "s_n", "s_tp", "s_tev", "s_av"))
        m_ohi, m_olo = sig("m_ohi", 2), sig("m_olo", 2)
        my_ps, mg_ps = sig("my_ps", 6), sig("mg_ps", 6)
        mg_th, mg_y, m_acc = sig("mg_th", 12), sig("mg_y", 12), sig("m_acc", 12)
        m_hi, m_lo = sig("m_hi", 4), sig("m_lo", 4)
        up_c0, up_c1, up_c = sig("up_c0", 2 * PAIRS), sig("up_c1", 2 * PAIRS), sig("up_c", 2 * PAIRS)
        f_gl, f_t, f_hi, f_lo = (sig(n, PAIRS) for n in ("f_gl", "f_t", "f_hi", "f_lo"))
        out_done = sem("out_done")

        GROUPS = 3 * D // BW
        G0 = 2 * D // BW

        def slot_in(j):
            return raw_in[j % RING]

        def product_done(eng, l, j):
            eng.wait_ge(blk_used.s, blk_used.at(l, RING + j + 1))

        def block_shape(t, j):
            _, k, cols = mixer_blocks[j]
            return t[:, j % RING, 0:k * cols].rearrange("p (k n) -> p k n", k=k)

        def kv_parts(t, j, packed):
            v = t[:, j % RING, :].bitcast(F32) if packed == "read" else t[:, j % RING, :]
            if packed:
                v = v.rearrange("p (k two h n) -> p k two h n", k=KVK, two=2, h=HEADS)
                return [v[:, :, i] for i in range(2)]
            v = v.rearrange("p (k h two n) -> p k h two n", k=KVK, two=2, h=HEADS)
            return [v[:, :, :, i] for i in range(2)]

        def ffn_shape(t, slot, kind):
            k = 2 if kind == "down" else DK
            return t[:, slot, :].rearrange("p (k n) -> p k n", k=k)

        blk = ctx.enter_context(nc.Block())

        @blk.sync
        def _(sp):
            c_dram = A["c"].rearrange("o (p k) -> p (o k)", p=P)
            sp.dma_start(cact[:], c_dram).then_inc(c_in, 16)
            sp.dma_start(pos_i, A["positions"][0, :].partition_broadcast(P)).then_inc(pos_in, 16)
            ada0 = A["ada_w"][0].rearrange("(p k) n -> p k n", p=P)
            for g in range(G0):
                if g >= 2:
                    sp.wait_ge(ada0_done, g - 1)
                dst = (AB, CD)[g % 2]
                sp.dma_start(dst[:], ada0[:, :, BW * g:BW * g + BW]).then_inc(ada_in[g % 2], 16)
                if g == 1:
                    sp.dma_start(cst[:], consts).then_inc(cst_in, 16)
                    sp.dma_start(x[:], A["x"].rearrange("o (c p) d -> p (o c) d", p=P)).then_inc(x_in, 16)

            with sp.Fori(0, L) as l:
                for j, (src, k, cols) in enumerate(mixer_blocks):
                    sp.wait_ge(lo_ready.s, lo_ready.at(l, RING + previous(j) + 1))
                    sp.sem_inc(sp_tick, 1)
                    sp.dma_start(block_shape(raw, j), src(l)).then_inc(slot_in(j).s, 16)
                    if j == 4:
                        sp.wait_ge(wbd_zero.s, wbd_zero.at(l, 1))
                        sp.sem_inc(sp_tick, 1)
                        for m, name in enumerate(("lru_wa", "lru_wx")):
                            for i in range(4):
                                for b in range(2):
                                    blockw = A[name][bass.ds(l, 1)].rearrange("a n h k -> (a n) h k")[2 * i + b]
                                    sp.dma_start(wbd[64 * b:64 * b + 64, m, i, 64 * b:64 * b + 64],
                                                 blockw).then_inc(wbd_in.s, 16)

                def up(l, c0, n):
                    return A["ffn_w_up"][bass.ds(l, 1)].rearrange("a (k p) n -> p (a k) n", p=P)[:, :, bass.ds(c0, n)]

                def load(j_wait, slot, kind, src):
                    sp.wait_ge(lo_ready.s, lo_ready.at(l, j_wait))
                    sp.sem_inc(sp_tick, 1)
                    sp.dma_start(ffn_shape(raw, slot, kind), src).then_inc(raw_in[slot].s, 16)

                load(NM + 1, NM % RING, "up", up(l, 0, BW))
                load(NM + 2, (NM + 1) % RING, "up", up(l, FF, BW))
                with sp.Fori(1, PAIRS) as i:
                    load(3 * i + NM, (NM + 2) % RING, "up", up(l, i * BW, BW))
                    load(3 * i + NM + 1, NM % RING, "up", up(l, i * BW + FF, BW))
                    down = A["ffn_w_down"][bass.ds(l, 1)].rearrange("a (k p) n -> p (a k) n", p=P)
                    load(3 * i + NM + 2, (NM + 1) % RING, "down", down[:, bass.ds(2 * i - 2, 2), :])
                down = A["ffn_w_down"][bass.ds(l, 1)].rearrange("a (k p) n -> p (a k) n", p=P)
                load(NB, (NM + 2) % RING, "down", down[:, 2 * PAIRS - 2:2 * PAIRS, :])

            out_v = out.rearrange("o (c p) d -> p (o c) d", p=P)
            for c in range(TC):
                sp.wait_ge(x_ready.s, x_ready.at(L, c + 1))
                sp.dma_start(out_v[:, c, :], x[:, c, :]).then_inc(out_done, 16)
            sp.wait_ge(out_done, 16 * TC)

        @blk.gpsimd
        def _(pool):
            pool.sem_inc(lo_ready.s, RING)
            pool.sem_inc(blk_used.s, RING)
            pool.sem_inc(ada_sum, 2)
            nc.gpsimd.memset(par[:], 0.0).then_inc(par_zero, 1)
            pool.wait_ge(cact_ready, 1)

            def ada_groups(src, first, count):

                def load(g, half):
                    pool.dma_start(adw[:, half], src(g)[:, 4 * half:4 * half + 4, :]).then_inc(adw_in[half], 16)

                load(0, 0)
                load(0, 1)
                def two_groups(it, last):
                    for b in range(2):
                        g = it * 2 + b
                        n = g + first
                        for half in range(2):
                            weights = adw[:, half]
                            cb = cact[:, 4 * half:4 * half + 4].unsqueeze(2).to_broadcast([P, 4, BW])
                            pool.wait_ge(adw_in[half], n * 16 + 16)
                            nc.gpsimd.tensor_tensor(adp[:], weights, cb, ALU.mult).then_inc(ad_op, 1)
                            pool.wait_ge(ad_op, n * 8 + 4 * half + 1)
                            pool.sem_inc(tick, 1)
                            if b == 0 or not last:
                                load(g + 1, half)
                            nc.gpsimd.tensor_tensor(adp[:, 0:2], adp[:, 0:2], adp[:, 2:4], ALU.add).then_inc(ad_op, 1)
                            pool.wait_ge(ad_op, n * 8 + 4 * half + 2)
                            if half == 0:
                                pool.wait_ge(ada_sum, n + 1)
                                nc.gpsimd.tensor_tensor(adacc[:, b], adp[:, 0], adp[:, 1], ALU.add).then_inc(ad_op, 1)
                                pool.wait_ge(ad_op, n * 8 + 3)
                                pool.sem_inc(ad_op, 1)
                            else:
                                nc.gpsimd.tensor_tensor(adp[:, 0], adp[:, 0], adp[:, 1], ALU.add).then_inc(ad_op, 1)
                                pool.wait_ge(ad_op, n * 8 + 7)
                                nc.gpsimd.tensor_tensor(adacc[:, b], adacc[:, b], adp[:, 0], ALU.add).then_inc(acc_ready, 1)
                                pool.wait_ge(acc_ready, n + 1)
                                pool.sem_inc(ad_op, 1)

                with pool.Fori(0, count // 2 - 1) as it:
                    two_groups(it, False)
                two_groups(count // 2 - 1, True)

            def columns(l, base):
                v = A["ada_w"][bass.ds(l, 1)].rearrange("a (p k) n -> p (a k) n", p=P)
                return lambda g: v[:, :, bass.ds(g * BW + base, BW)]

            ada_groups(columns(0, G0 * BW), 0, GROUPS - G0)
            head = GROUPS - G0
            with pool.Fori(0, L - 1) as l:
                ada_groups(columns(l, 3 * D), l * 2 * GROUPS + head, GROUPS)
                ada_groups(columns(l + 1, 0), l * 2 * GROUPS + head + GROUPS, GROUPS)
            ada_groups(columns(L - 1, 3 * D), (L - 1) * 2 * GROUPS + head, GROUPS)
            pool.sem_inc(acc_ready, GROUPS)

        @blk.scalar
        def _(act):
            A_ = nc.scalar.activation
            rowbuf = tmp[:].rearrange("p a b -> p (a b)")[:, 0:L * 3 * P].rearrange("p (l c n) -> p l c n", l=L, c=3)
            n_rows = 0
            for ch, vecs in enumerate(layout):
                for name, cnt in vecs:
                    r0 = col[name] - ch * P
                    if name.startswith("tap"):
                        src = A["ffn_conv_w"][:, int(name[3]), :]
                    elif name == "lru_conv_w":
                        src = A[name].rearrange("l k n -> l (k n)")
                    else:
                        src = A[name]
                    act.dma_start(rowbuf[r0:r0 + cnt, :, ch, :],
                                  src.rearrange("l (r n) -> r l n", n=P)).then_inc(rows_in, 16)
                    n_rows += 1
            act.wait_ge(c_in, 16)
            A_(st[:, 0:DK], cact[:], ACT.Sigmoid).then_inc(sig_c, 1)
            act.wait_ge(cact_ready, 1)
            act.wait_ge(x_in, 16)
            act.sem_inc(x_ready.s, TC)
            act.wait_ge(ang_ready, 1)
            for n, (t, scale) in enumerate(((sinr, 1.0), (cosr, 1.0), (sinm, 1.0), (cosm, 1.0))):
                A_(t[:], t[:], ACT.Sin).then_inc(trig_ready, 1)
            act.wait_ge(sp_d, 2)
            A_(spt[:, 2], spt[:, 1], ACT.Exp, scale=-1.0).then_inc(sp_a, 1)
            act.wait_ge(sp_d, 3)
            A_(spt[:, 4], spt[:, 3], ACT.Ln).then_inc(sp_a, 1)

            def split_hi(l, j, dst, src):
                act.wait_ge(slot_in(j).s, slot_in(j).at(l, 16 * (j // RING + 1)))
                act.wait_ge(blk_used.s, blk_used.at(l, RING + previous(j) + 1))
                A_(dst, src, ACT.Copy).then_inc(hi_ready.s, 1)

            def split_block(l, j):
                if j == J[("c", 2)]:
                    r = block_shape(raw, j)
                    d = w_hi[:, j % RING, :].rearrange("p (k n) -> p k n", k=DK)
                    act.wait_ge(slot_in(j).s, slot_in(j).at(l, 16 * (j // RING + 1)))
                    act.wait_ge(blk_used.s, blk_used.at(l, RING + previous(j) + 1))
                    A_(d[:, :, 0:P], r[:, :, 0:P], ACT.Copy)
                    A_(d[:, :, P:2 * P].rearrange("p k (q n) -> p k q n", q=4),
                       r[:, :, P:P + 32].unsqueeze(2).to_broadcast([P, DK, 4, 32]), ACT.Copy).then_inc(hi_ready.s, 1)
                elif j == J[("ukv", 0)]:
                    act.wait_ge(slot_in(j).s, slot_in(j).at(l, 16 * (j // RING + 1)))
                    act.wait_ge(blk_used.s, blk_used.at(l, RING + previous(j) + 1))
                    for d, r in zip(kv_parts(w_hi, j, True), kv_parts(raw, j, False)):
                        a = A_(d, r, ACT.Copy)
                    a.then_inc(hi_ready.s, 1)
                elif j < NM:
                    split_hi(l, j, block_shape(w_hi, j), block_shape(raw, j))
                else:
                    split_hi(l, j, w_hi[:, j % RING, :], raw[:, j % RING, :])

            def half_start(l, ph, first):
                for c in range(TC):
                    n = 2 * ph + c
                    act.wait_ge(x_ready.s, x_ready.at(l, n + 1))
                    if c == 1:
                        act.wait_ge(par_ready, 6)
                    junk = (lat, tmp)[c][:].rearrange("p a b -> p (a b)")[:, 0:D]
                    A_(junk, x[:, c, :], ACT.Square, accum_out=st[:, c:c + 1]).then_inc(n_ss.s, 1)
                    act.wait_ge(n_ss.s, n_ss.at(l, n + 1))
                    A_(st[:, 2 + c:3 + c], st[:, c:c + 1], ACT.Sqrt, scale=1.0 / D, bias=eps).then_inc(n_sq.s, 1)
                split_block(l, first)
                act.wait_ge(mod_ready.s, mod_ready.at(l, 2 * ph + 2))
                for c in range(TC):
                    n = 2 * ph + c
                    bank = (4, 0)[c]
                    cs = slice(P * c, P * c + P)
                    act.wait_ge(n_tp.s, n_tp.at(l, 2 * n + 1))
                    for k in range(4):
                        a = A_(h32[:, k, cs], PS[:, bank, P * k:P * k + P], ACT.Identity,
                               scale=hscale[:, k:k + 1], bias=mod[:, k:k + 1])
                    a.then_inc(n_ha.s, 1)
                    act.wait_ge(n_ha.s, n_ha.at(l, n + 1))
                    act.wait_ge(n_hd.s, n_hd.at(l, n + 1))
                    A_(h_hi[:, :, cs], h32[:, :, cs], ACT.Copy).then_inc(n_hi.s, 1)
                    split_block(l, first + 1 + c)
                for i in range(2):
                    act.wait_ge(grow_ps.s, grow_ps.at(l, 2 * ph + i + 1))
                    A_(grow[:, 512 * i:512 * i + 512], PS[:, (6, 3)[i], :], ACT.Copy).then_inc(grow_ev.s, 1)

            def half_end(l, ph):
                for c in range(TC):
                    n = 2 * ph + c
                    if c == 0:
                        act.wait_ge(y_ps.s, y_ps.at(l, ph + 1))
                    else:
                        product_done(act, l, NM - 1 if ph == 0 else NB - 1)
                    junk = (CD, AB)[c][:].rearrange("p a b -> p (a b)")[:, 0:D]
                    A_(junk, PS[:, 2 * c:2 * c + 2, :].rearrange("p a b -> p (a b)"), ACT.Square,
                       accum_out=st[:, 6 + c:7 + c]).then_inc(p_ss.s, 1)
                    act.wait_ge(p_ss.s, p_ss.at(l, n + 1))
                    A_(st[:, 8 + c:9 + c], st[:, 6 + c:7 + c], ACT.Sqrt, scale=1.0 / D, bias=eps).then_inc(p_sq.s, 1)

            def flat2(t, i):
                return t[:, 2 * i:2 * i + 2, :].rearrange("p a b -> p (a b)")

            with act.Fori(0, L) as l:
                half_start(l, 0, 0)
                for i in range(4):
                    product_done(act, l, i)
                    A_(flat2(AB, i), PS[:, (2, 4, 5, 0)[i], :], ACT.Copy).then_inc(qk_ev.s, 1)
                    split_block(l, i + 3)
                split_block(l, 7)
                product_done(act, l, J[("v", 1)])
                for c in range(TC):
                    A_(flat2(CD, c), PS[:, (1, 3)[c], :], ACT.Copy).then_inc(v_ev.s, 1)
                split_block(l, 8)
                for i in range(2):
                    product_done(act, l, J[("g", i)])
                    A_(flat2(CD, 2 + i), PS[:, (4, 1)[i], :], ACT.Tanh, scale=0.5).then_inc(g_th.s, 1)
                    split_block(l, 9 + i)
                for i in range(2):
                    product_done(act, l, J[("lx", i)])
                    for t in (2 * i, 2 * i + 1):
                        a = A_(EF[:, t, :], PS[:, (3, 6)[i], T * (t % 2):T * (t % 2) + T], ACT.Identity,
                               scale=pc("lru_conv_w", 12 + t), bias=pc("lru_conv_b", t))
                    a.then_inc(lx_c0.s, 1)
                    split_block(l, 11 + i)
                for i in range(2):
                    product_done(act, l, J[("lg", i)])
                    A_(flat2(EF, 2 + i), PS[:, (2, 4)[i], :], ACT.Gelu_apprx_tanh).then_inc(lg_ev.s, 1)
                    split_block(l, 13 + i)
                product_done(act, l, J[("c", 0)])
                A_(flat2(lat, 0), PS[:, 5, :], ACT.Copy)
                A_(flat2(tmp, 0), PS[:, 5, :], ACT.Square)
                split_block(l, 15)
                product_done(act, l, J[("c", 1)])
                A_(flat2(lat, 1), PS[:, 0, :], ACT.Copy)
                A_(flat2(tmp, 1), PS[:, 0, :], ACT.Square)
                split_block(l, 16)
                product_done(act, l, J[("c", 2)])
                A_(lat[:, 4, :], PS[:, 1, 0:T], ACT.Copy).then_inc(c_ev.s, 1)
                A_(tmp[:, 4, :], PS[:, 1, 0:T], ACT.Square).then_inc(c_sq.s, 1)
                A_(kr[:], PS[:, 1, T:2 * T], ACT.Copy).then_inc(kr_ev.s, 1)
                split_block(l, 17)
                act.wait_ge(cs_ps.s, cs_ps.at(l, 1))
                A_(rs2[:, 0, :], PS[:, 2, 0:T], ACT.Sqrt, scale=1.0 / QR, bias=eps)
                A_(rs2[:, 1, :], PS[:, 2, T:2 * T], ACT.Sqrt, scale=1.0 / KVR, bias=eps).then_inc(cs_sd.s, 1)
                for i in range(2):
                    act.wait_ge(rs_av.s, rs_av.at(l, 4 * i + 4))
                    A_(flat2(AB, i), PS[:, (3, 5)[i], :], ACT.Copy).then_inc(ry_ev.s, 1)
                act.wait_ge(cn.s, cn.at(l, 2))
                A_(ob_hi[:], lat[:], ACT.Copy).then_inc(cn_hi.s, 1)
                for i in range(2):
                    act.wait_ge(ry_ps.s, ry_ps.at(l, i + 1))
                    A_(flat2(tmp, i), PS[:, (0, 1)[i], :], ACT.Square).then_inc(rv_sq.s, 1)
                for i in range(2):
                    act.wait_ge(rv_ps.s, rv_ps.at(l, i + 1))
                    A_(flat2(AB, 2 + i), PS[:, (2, 3)[i], :], ACT.Sqrt, bias=eps).then_inc(rv_sd.s, 1)
                for i in range(2):
                    act.wait_ge(r_o.s, r_o.at(l, i + 1))
                    A_(flat2(oa_hi, i), flat2(CD, i), ACT.Copy).then_inc(r_ohi.s, 1)
                for i in range(4):
                    act.wait_ge(lr_ps.s, lr_ps.at(l, i + 1))
                    if i == 0:
                        act.wait_ge(r_yn.s, r_yn.at(l, 2))
                    for b in range(2):
                        t = 2 * (i % 2) + b
                        dst = AB[:, 4 + t, :] if i < 2 else AB[:, t, :]
                        a = A_(dst, PS[:, (5, 6, 4, 0)[i], T * b:T * b + T], ACT.Sigmoid,
                               bias=pc("lru_ba" if i < 2 else "lru_bx", t))
                    if i % 2:
                        a.then_inc(lr_ev.s, 1)
                act.wait_ge(lr_ev.s, lr_ev.at(l, 1))
                act.wait_ge(r_olo.s, r_olo.at(l, 2))
                act.wait_ge(r_ohi.s, r_ohi.at(l, 2))
                for t in range(4):
                    a = A_(CD[:, 4 + t, :], AB[:, 4 + t, :], ACT.Tanh, scale=pc("8sp", t))
                a.then_inc(l_at.s, 1)
                for t in range(4):
                    a = A_(CD[:, t, :], AB[:, 4 + t, :], ACT.Exp, scale=pc("-8sp", t))
                a.then_inc(l_at.s, 1)
                act.wait_ge(l_v.s, l_v.at(l, 2))
                A_(CD[:, 4:8, :], CD[:, 4:8, :], ACT.Sqrt).then_inc(l_mult.s, 1)
                act.wait_ge(l_u.s, l_u.at(l, 1))
                act.wait_ge(l_h.s, l_h.at(l, 4))
                for i in range(4):
                    if i % 2 == 0:
                        act.wait_ge(uq_ps.s, uq_ps.at(l, i // 2 + 1))
                    else:
                        product_done(act, l, J[("uq", i // 2)])
                    A_(AB[0:DQK, 2 * i:2 * i + 2, :].rearrange("p a b -> p (a b)"), PS[0:DQK, (2, 3, 5, 6)[i], :],
                       ACT.Copy).then_inc(uq_ev.s, 1)
                    if i % 2:
                        split_block(l, 18 + i // 2)
                act.wait_ge(l_o.s, l_o.at(l, 1))
                for i in range(2):
                    act.wait_ge(uk_ps.s, uk_ps.at(l, i + 1))
                    for b in range(2):
                        dst = CD[0:64, 4 * i + b:4 * i + b + 3:2, :]
                        a = A_(dst, PS[64 * b:64 * b + 64, (4, 0)[i], :].rearrange("p (a b) -> p a b", a=2), ACT.Copy)
                    a.then_inc(uk_ev.s, 1)
                for c in range(TC):
                    if c == 0:
                        act.wait_ge(uv_ps.s, uv_ps.at(l, 1))
                    else:
                        product_done(act, l, J[("ukv", 0)])
                    A_(flat2(EF, c), PS[:, (1, 2)[c], :], ACT.Copy).then_inc(uv_ev.s, 1)
                split_block(l, 20)
                act.wait_ge(cn_lo.s, cn_lo.at(l, 1))
                A_(ob_hi[:, 0:4, :], EF[:, 4:8, :], ACT.Copy).then_inc(l_ohi.s, 1)

                def gate(m):
                    if m % 2 == 0:
                        product_done(act, l, J[("gate", m // 4, m % 4)])
                    else:
                        act.wait_ge(mg_ps.s, mg_ps.at(l, m // 2 + 1))
                    if m >= 2:
                        act.wait_ge(mg_y.s, mg_y.at(l, m - 1))
                    A_(flat2(lat, m % 2), PS[:, (4, 6)[m % 2], :], ACT.Tanh, scale=0.5).then_inc(mg_th.s, 1)

                def softmax_exp(h):
                    act.wait_ge(s_neg.s, s_neg.at(l, h + 1))
                    pb = pbuf[:, h % 2, :]
                    A_(pb[:, 0:P], pb[:, 0:P], ACT.Exp, bias=mx[:, h % 2, 2:3], accum_out=mx[:, h % 2, 4:5])
                    A_(pb[:, P:3 * P], pb[:, P:3 * P], ACT.Exp, bias=mx[:, h % 2, 3:4],
                       accum_out=mx[:, h % 2, 5:6]).then_inc(s_e.s, 1)

                def transposed(h):
                    act.wait_ge(s_tp.s, s_tp.at(l, h + 1))
                    if h >= 2:
                        act.wait_ge(s_av.s, s_av.at(l, h - 1))
                    A_(ptb[:, h % 2, :], PS[:, 1, 0:384], ACT.Copy).then_inc(s_tev.s, 1)

                def attended(i):
                    act.wait_ge(s_av.s, s_av.at(l, 4 * i + 4))
                    if i == 0:
                        product_done(act, l, J[("gate", 0, 3)])
                    A_(flat2(oa_hi, i), PS[:, 2, :], ACT.Copy).then_inc(m_ohi.s, 1)

                def merged_hi(i):
                    act.wait_ge(m_acc.s, m_acc.at(l, 9 + i))
                    if i == 0:
                        product_done(act, l, J[("gate", 1, 3)])
                    if i == 2:
                        product_done(act, l, J[("gate", 2, 3)])
                    A_(flat2(ob_hi if i < 2 else oa_hi, i % 2), flat2(h32, i), ACT.Copy, scale=0.5).then_inc(m_hi.s, 1)

                softmax_exp(0)
                for m in range(12):
                    j = J[("gate", 0, 0)] + 3 * (m // 2)
                    if m < HEADS - 1:
                        softmax_exp(m + 1)
                    gate(m)
                    if m < HEADS:
                        transposed(m)
                    if m % 2 == 0:
                        split_block(l, j + RING)
                    else:
                        split_block(l, j + RING + 1)
                        split_block(l, j + RING + 2)
                    if m in (3, 7):
                        attended(m // 4)
                    if m in (8, 9):
                        merged_hi(m - 8)
                merged_hi(2)
                merged_hi(3)
                for j in range(39, NM):
                    split_block(l, j)
                half_end(l, 0)

                half_start(l, 1, NM)

                def conv(n, part, i, first=False):
                    product_done(act, l, NM + part if first else i * 3 + (NM - 1 + part))
                    if not first:
                        act.wait_ge(f_t.s, f_t.at(l, i))
                    for b in range(2):
                        a = A_(EF[:, 2 * part + b, :], PS[:, 4 + part, T * b:T * b + T], ACT.Identity,
                               scale=cur[:, bass.ds(i * 2 + col["tap2"] + NFF * part + b, 1)],
                               bias=cur[:, bass.ds(i * 2 + col["ffn_conv_b"] + NFF * part + b, 1)])
                    a.then_inc(up_c0.s, 1)

                def gelu(i):
                    act.wait_ge(up_c.s, up_c.at(l, i * 2 + 2))
                    A_(flat2(EF, 1), flat2(EF, 1), ACT.Gelu_apprx_tanh).then_inc(f_gl.s, 1)

                def hidden_hi(i):
                    act.wait_ge(f_t.s, f_t.at(l, i + 1))
                    A_(flat2(oa_hi, 0), flat2(tmp, 0), ACT.Copy).then_inc(f_hi.s, 1)

                def ffn_split(i, part):
                    slot = (NM + 2 + part) % RING
                    j = i * 3 + (NM + 2 + part)
                    uses = i + (NM + 2 + part) // RING
                    act.wait_ge(raw_in[slot].s, raw_in[slot].at(l, uses * 16 + 16))
                    act.wait_ge(blk_used.s, blk_used.at(l, j + 1))
                    A_(w_hi[:, slot, :], raw[:, slot, :], ACT.Copy).then_inc(hi_ready.s, 1)

                conv(0, 0, 0, first=True)
                split_block(l, NM + 3)
                conv(1, 1, 0, first=True)
                split_block(l, NM + 4)
                gelu(0)
                hidden_hi(0)
                with act.Fori(1, PAIRS - 1) as i:
                    conv(i * 2, 0, i)
                    ffn_split(i, 0)
                    conv(i * 2 + 1, 1, i)
                    ffn_split(i, 1)
                    gelu(i)
                    ffn_split(i, 2)
                    product_done(act, l, i * 3 + (NM + 1))
                    hidden_hi(i)
                i = PAIRS - 1
                conv(i * 2, 0, i)
                ffn_split(i, 0)
                conv(i * 2 + 1, 1, i)
                gelu(i)
                product_done(act, l, i * 3 + (NM + 1))
                hidden_hi(i)
                half_end(l, 1)

        @blk.vector
        def _(dve):
            V = nc.vector
            st_n = [0]

            def step(ins):
                st_n[0] += 1
                ins.then_inc(pro, 1)
                dve.wait_ge(pro, st_n[0])

            PI = 3.1415925
            TWO_PI = 6.283185307179586
            PARTS = (6.28125, 2029 / 2 ** 20)
            REST = TWO_PI - PARTS[0] - PARTS[1]
            MAGIC = 12582912.0
            dve.wait_ge(pos_in, 16)
            dve.wait_ge(cst_in, 16)
            step(V.tensor_copy(rs2[:, 0], pos_i))
            for s, c, inv in ((sinr, cosr, inv_ret), (sinm, cosm, inv_mla)):
                step(V.tensor_scalar(s[:], rs2[:, 0], inv, None, ALU.mult))
                step(V.tensor_scalar(rs2[:, 1], s[:], 1.0 / TWO_PI, MAGIC, ALU.mult, ALU.add))
                step(V.tensor_scalar(rs2[:, 1], rs2[:, 1], MAGIC, None, ALU.subtract))
                for part in (*PARTS, REST):
                    step(V.scalar_tensor_tensor(s[:], rs2[:, 1], -part, s[:], ALU.mult, ALU.add))
                step(V.tensor_scalar(c[:], s[:], PI / 2, TWO_PI, ALU.is_gt, ALU.mult))
                step(V.scalar_tensor_tensor(c[:], s[:], TWO_PI / 4, c[:], ALU.add, ALU.subtract))
                step(V.tensor_scalar(c[:], c[:], PI, -PI, ALU.min, ALU.max))
                step(V.tensor_scalar(s[:], s[:], PI, -PI, ALU.min, ALU.max))
            V.memset(st[:, 12:16], 0.0).then_inc(ang_ready, 1)

            dve.wait_ge(sig_c, 1)
            V.tensor_tensor(cact[:], cact[:], st[:, 0:DK], ALU.mult).then_inc(cact_ready, 1)
            dve.wait_ge(cact_ready, 1)

            for g in range(G0):
                dve.wait_ge(ada_in[g % 2], 16 * (g // 2 + 1))
                wbuf = (AB, CD)[g % 2]
                step(V.tensor_scalar(h32[:, g, :], wbuf[:, 0, :], cact[:, 0:1], None, ALU.mult))
                for k in range(1, DK - 1):
                    step(V.scalar_tensor_tensor(h32[:, g, :], wbuf[:, k, :], cact[:, k:k + 1], h32[:, g, :],
                                                ALU.mult, ALU.add))
                V.scalar_tensor_tensor(h32[:, g, :], wbuf[:, DK - 1, :], cact[:, DK - 1:DK], h32[:, g, :],
                                       ALU.mult, ALU.add).then_inc(ada0_done, 1)
                dve.wait_ge(ada0_done, g + 1)

            dve.wait_ge(par_zero, 1)
            for n in range(3 * L):
                l0, ch = n // 3, n % 3
                dve.wait_ge(par_ps, n + 1)
                V.tensor_copy(par[:, l0, P * ch:P * ch + used[ch]], PS[:, n, 0:used[ch]]).then_inc(par_ready, 1)
            dve.wait_ge(par_ready, 3 * L)
            for l0 in range(L):
                step(V.tensor_copy(spt[:, 0, WK * l0:WK * l0 + WK], par[:, l0, col["lru_lambda"]:col["lru_lambda"] + WK]))
            V.tensor_scalar(spt[:, 5], spt[:, 0], -1.0, None, ALU.mult).then_inc(sp_d, 1)
            dve.wait_ge(sp_d, 1)
            V.tensor_tensor(spt[:, 1], spt[:, 0], spt[:, 5], ALU.max).then_inc(sp_d, 1)
            dve.wait_ge(sp_a, 1)
            V.tensor_scalar(spt[:, 3], spt[:, 2], 1.0, None, ALU.add).then_inc(sp_d, 1)
            dve.wait_ge(sp_d, 3)
            step(V.tensor_scalar(spt[:, 6], spt[:, 3], 1.0, None, ALU.subtract))
            step(V.tensor_tensor(spt[:, 6], spt[:, 2], spt[:, 6], ALU.subtract))
            step(V.reciprocal(spt[:, 7], spt[:, 3]))
            step(V.tensor_tensor(spt[:, 6], spt[:, 6], spt[:, 7], ALU.mult))
            step(V.scalar_tensor_tensor(spt[:, 6], spt[:, 5], 0.0, spt[:, 6], ALU.max, ALU.add))
            dve.wait_ge(sp_a, 2)
            step(V.tensor_tensor(spt[:, 6], spt[:, 6], spt[:, 4], ALU.add))
            for l0 in range(L):
                for name, sign in (("-8sp", -LRU_C), ("8sp", LRU_C)):
                    step(V.tensor_scalar(par[:, l0, col[name]:col[name] + WK], spt[:, 6, WK * l0:WK * l0 + WK], sign,
                                         None, ALU.mult))

            def split_lo(l, j, dst, whole, hi):
                dve.wait_ge(hi_ready.s, hi_ready.at(l, j + 1))
                V.tensor_tensor(dst, whole, hi, ALU.subtract).then_inc(lo_ready.s, 1)

            def split_block(l, j):
                if j == J[("c", 2)]:
                    r = block_shape(raw, j)
                    h = w_hi[:, j % RING, :].bitcast(F32).rearrange("p (k n) -> p k n", k=DK)
                    d = w_lo[:, j % RING, :].rearrange("p (k n) -> p k n", k=DK)
                    dve.wait_ge(hi_ready.s, hi_ready.at(l, j + 1))
                    V.tensor_tensor(d[:, :, 0:P], r[:, :, 0:P], h[:, :, 0:P], ALU.subtract)
                    V.tensor_tensor(d[:, :, P:2 * P].rearrange("p k (q n) -> p k q n", q=4),
                                    r[:, :, P:P + 32].unsqueeze(2).to_broadcast([P, DK, 4, 32]),
                                    h[:, :, P:2 * P].rearrange("p k (q n) -> p k q n", q=4),
                                    ALU.subtract).then_inc(lo_ready.s, 1)
                elif j == J[("ukv", 0)]:
                    dve.wait_ge(hi_ready.s, hi_ready.at(l, j + 1))
                    for d, r, h in zip(kv_parts(w_lo, j, True), kv_parts(raw, j, False), kv_parts(w_hi, j, "read")):
                        v = V.tensor_tensor(d, r, h, ALU.subtract)
                    v.then_inc(lo_ready.s, 1)
                elif j < NM:
                    _, k, cols = mixer_blocks[j]
                    n = k * cols
                    s = j % RING
                    split_lo(l, j, w_lo[:, s, 0:n], raw[:, s, 0:n], w_hi[:, s, 0:n].bitcast(F32))
                else:
                    s = j % RING
                    split_lo(l, j, w_lo[:, s, :], raw[:, s, :], w_hi[:, s, :].bitcast(F32))

            def half_start(l, ph, first):
                for c in range(TC):
                    n = 2 * ph + c
                    dve.wait_ge(n_sq.s, n_sq.at(l, n + 1))
                    V.reciprocal(st[:, 4 + c:5 + c], st[:, 2 + c:3 + c]).then_inc(n_rs.s, 1)
                    dve.wait_ge(n_rs.s, n_rs.at(l, n + 1))
                    dst = (AB, CD)[c][:].rearrange("p a b -> p (a b)")[:, D:2 * D]
                    V.tensor_scalar(dst, x[:, c, :], st[:, 4 + c:5 + c], None, ALU.mult).then_inc(n_xn.s, 1)
                    if c == 0:
                        if ph == 0:
                            V.tensor_copy(cur[:], par[:, bass.ds(l, 1), :].rearrange("p a b -> p (a b)")).then_inc(cur_ready.s, 1)
                            dve.wait_ge(cur_ready.s, cur_ready.at(l, 1))
                        dve.wait_ge(ada0_sum, 1)
                        dve.wait_ge(ada_sum, l * 2 * GROUPS + (2 + GROUPS - G0 + GROUPS * ph))
                        V.tensor_tensor(mod[:], PS[:, ADA_BANK, 0:24], pc("ada_b", 24 * ph, 24), ALU.add).then_inc(mod_evac.s, 1)
                        dve.wait_ge(mod_evac.s, mod_evac.at(l, ph + 1))
                        pre, post = ("mix_pre_g", "mix_post_g") if ph == 0 else ("ffn_pre_g", "ffn_post_g")
                        V.tensor_tensor(gcol[:], mod[:, 16:24], pc(post, 0, DK), ALU.mult).then_inc(mod_ready.s, 1)
                        V.scalar_tensor_tensor(hscale[:], mod[:, 8:16], 1.0, pc(pre, 0, DK), ALU.add, ALU.mult).then_inc(mod_ready.s, 1)
                        dve.wait_ge(mod_ready.s, mod_ready.at(l, 2 * ph + 2))
                split_block(l, first)
                for c in range(TC):
                    n = 2 * ph + c
                    bank = (5, 1)[c]
                    cs = slice(P * c, P * c + P)
                    dve.wait_ge(n_tp.s, n_tp.at(l, 2 * n + 2))
                    for k in range(4, DK):
                        v = V.tensor_scalar(h32[:, k, cs], PS[:, bank, P * (k - 4):P * (k - 3)],
                                            hscale[:, k:k + 1], mod[:, k:k + 1], ALU.mult, ALU.add)
                    v.then_inc(n_hd.s, 1)
                    dve.wait_ge(n_hi.s, n_hi.at(l, n + 1))
                    V.tensor_tensor(h_lo[:, :, cs], h32[:, :, cs], h_hi[:, :, cs].bitcast(F32), ALU.subtract).then_inc(n_lo.s, 1)
                    split_block(l, first + 1 + c)

            def half_end(l, ph):
                dve.wait_ge(grow_ev.s, grow_ev.at(l, 2 * ph + 2))
                for c in range(TC):
                    n = 2 * ph + c
                    dve.wait_ge(p_sq.s, p_sq.at(l, n + 1))
                    V.reciprocal(st[:, 10 + c:11 + c], st[:, 8 + c:9 + c]).then_inc(p_rs.s, 1)
                    dve.wait_ge(p_rs.s, p_rs.at(l, n + 1))
                    y = (CD, AB)[c][:].rearrange("p a b -> p (a b)")[:, D:2 * D]
                    V.scalar_tensor_tensor(y, PS[:, 2 * c:2 * c + 2, :].rearrange("p a b -> p (a b)"),
                                           st[:, 10 + c:11 + c], grow[:], ALU.mult, ALU.mult).then_inc(p_y.s, 1)
                    dve.wait_ge(p_y.s, p_y.at(l, n + 1))
                    V.tensor_tensor(x[:, c, :], x[:, c, :], y, ALU.add).then_inc(x_ready.s, 1)

            def flat2(t, i):
                return t[:, 2 * i:2 * i + 2, :].rearrange("p a b -> p (a b)")

            def twice(t):
                return t[:].unsqueeze(1).to_broadcast([P, 2, T])

            dve.wait_ge(trig_ready, 4)
            with dve.Fori(0, L) as l:
                half_start(l, 0, 0)
                V.memset(wbd[:], 0.0).then_inc(wbd_zero.s, 1)

                def rope_pair(i):
                    dve.wait_ge(rot_ps.s, rot_ps.at(l, i + 1))
                    two = tmp[:, 2 * (i % 2):2 * (i % 2) + 2, :]
                    ps = PS[:, (6, 2, 5, 0)[i], :].rearrange("p (a b) -> p a b", a=2)
                    V.tensor_tensor(two, ps, twice(sinr), ALU.mult).then_inc(rot_t.s, 1)
                    V.tensor_tensor(AB[:, 2 * i:2 * i + 2, :], AB[:, 2 * i:2 * i + 2, :], twice(cosr), ALU.mult).then_inc(rot_c.s, 1)
                    dve.wait_ge(rot_t.s, rot_t.at(l, i + 1))
                    dve.wait_ge(rot_c.s, rot_c.at(l, i + 1))
                    V.tensor_tensor(AB[:, 2 * i:2 * i + 2, :], AB[:, 2 * i:2 * i + 2, :], two, ALU.add).then_inc(rope.s, 1)

                for j in range(3, 7):
                    split_block(l, j)
                split_block(l, 7)
                rope_pair(0)
                rope_pair(1)
                split_block(l, 8)
                for i in range(2):
                    dve.wait_ge(g_th.s, g_th.at(l, i + 1))
                    V.scalar_tensor_tensor(flat2(CD, 2 + i), flat2(CD, 2 + i), 1.0, PS[:, (4, 1)[i], :], ALU.add,
                                           ALU.mult).then_inc(g_ev.s, 1)
                    rope_pair(2 + i)
                    split_block(l, 9 + i)

                def ret_scores(h):
                    dve.wait_ge(rs_ps.s, rs_ps.at(l, h + 1))
                    if h >= 2:
                        dve.wait_ge(rs_av.s, rs_av.at(l, h - 1))
                    b = (2, 4)[h % 2]
                    V.tensor_tensor(pbuf[:, h % 2, 0:T], PS[:, b, 0:T], decay[:, h, :], ALU.mult)
                    V.tensor_tensor(pbuf[:, h % 2, T:T + P], PS[:, b, T:T + P], decay[:, h, 0:P], ALU.mult).then_inc(rs_p.s, 1)

                def lru_taps(i):
                    dve.wait_ge(lx_c0.s, lx_c0.at(l, i + 1))
                    for tap in range(3):
                        d = 3 - tap
                        for b in range(2):
                            t = 2 * i + b
                            if tap > 0:
                                dve.wait_ge(lx_c.s, lx_c.at(l, 6 * i + 2 * tap - 1 + b))
                            V.scalar_tensor_tensor(EF[:, t, d:T], PS[:, (3, 6)[i], T * b:T * b + T - d],
                                                   pc("lru_conv_w", 4 * tap + t), EF[:, t, d:T], ALU.mult,
                                                   ALU.add).then_inc(lx_c.s, 1)

                for i in range(2):
                    lru_taps(i)
                    split_block(l, 11 + i)
                split_block(l, 13)
                split_block(l, 14)
                for h in range(2):
                    ret_scores(h)
                split_block(l, 15)
                for h in range(2, 4):
                    ret_scores(h)
                split_block(l, 16)
                for h in range(4, 6):
                    ret_scores(h)
                split_block(l, 17)
                for h in range(6, 8):
                    ret_scores(h)
                dve.wait_ge(cs_sd.s, cs_sd.at(l, 1))
                V.reciprocal(rs2, rs2).then_inc(cs_rc.s, 1)
                dve.wait_ge(cs_rc.s, cs_rc.at(l, 1))
                dve.wait_ge(c_ev.s, c_ev.at(l, 1))
                for i in range(5):
                    gain = pc("mla_q_norm_g", i) if i < QK else pc("mla_kv_norm_g", i - QK)
                    v = V.scalar_tensor_tensor(lat[:, i, :], lat[:, i, :], gain, rs2[:, 0 if i < QK else 1], ALU.mult, ALU.mult)
                    if i in (2, 4):
                        v.then_inc(cn.s, 1)
                dve.wait_ge(cn_hi.s, cn_hi.at(l, 1))
                dve.wait_ge(cn.s, cn.at(l, 2))
                V.tensor_tensor(ob_lo[:], lat[:], ob_hi[:].bitcast(F32), ALU.subtract).then_inc(cn_lo.s, 1)
                for i in range(2):
                    dve.wait_ge(rv_sd.s, rv_sd.at(l, i + 1))
                    V.reciprocal(flat2(AB, 2 + i), flat2(AB, 2 + i)).then_inc(rv_rc.s, 1)
                    dve.wait_ge(rv_rc.s, rv_rc.at(l, i + 1))
                    V.scalar_tensor_tensor(flat2(CD, i), PS[:, (0, 1)[i], :], 0.5, flat2(AB, 2 + i), ALU.mult,
                                           ALU.mult).then_inc(r_yn.s, 1)
                    dve.wait_ge(r_yn.s, r_yn.at(l, i + 1))
                    V.tensor_tensor(flat2(CD, i), flat2(CD, i), flat2(CD, 2 + i), ALU.mult).then_inc(r_o.s, 1)
                for i in range(2):
                    dve.wait_ge(r_ohi.s, r_ohi.at(l, i + 1))
                    V.tensor_tensor(flat2(oa_lo, i), flat2(CD, i), flat2(oa_hi, i).bitcast(F32), ALU.subtract).then_inc(r_olo.s, 1)
                dve.wait_ge(l_at.s, l_at.at(l, 2))
                V.tensor_scalar(AB[:, 4:8, :], CD[:, 4:8, :], 1.0, None, ALU.add).then_inc(l_den.s, 1)
                dve.wait_ge(l_den.s, l_den.at(l, 1))
                V.reciprocal(AB[:, 4:8, :], AB[:, 4:8, :]).then_inc(l_rcp.s, 1)
                dve.wait_ge(lr_ev.s, lr_ev.at(l, 2))
                V.tensor_tensor(AB[:, 0:4, :], AB[:, 0:4, :], EF[:, 0:4, :], ALU.mult).then_inc(l_ix.s, 1)
                dve.wait_ge(l_rcp.s, l_rcp.at(l, 1))
                V.scalar_tensor_tensor(CD[:, 4:8, :], CD[:, 4:8, :], 2.0, AB[:, 4:8, :], ALU.mult, ALU.mult).then_inc(l_v.s, 1)
                dve.wait_ge(l_v.s, l_v.at(l, 1))
                V.tensor_scalar(CD[:, 4:8, :], CD[:, 4:8, :], TINY, None, ALU.max).then_inc(l_v.s, 1)
                dve.wait_ge(l_mult.s, l_mult.at(l, 1))
                dve.wait_ge(l_ix.s, l_ix.at(l, 1))
                V.tensor_tensor(AB[:, 0:4, :], AB[:, 0:4, :], CD[:, 4:8, :], ALU.mult).then_inc(l_u.s, 1)
                dve.wait_ge(l_u.s, l_u.at(l, 1))
                for t in range(4):
                    V.tensor_tensor_scan(EF[:, t, :], CD[:, t, :], AB[:, t, :], 0.0, ALU.mult, ALU.add).then_inc(l_h.s, 1)
                dve.wait_ge(l_h.s, l_h.at(l, 4))
                V.tensor_tensor(EF[:, 4:8, :], EF[:, 4:8, :], EF[:, 0:4, :], ALU.mult).then_inc(l_o.s, 1)
                RR = slice(64, 96)
                dve.wait_ge(kt_ps.s, kt_ps.at(l, 1))
                dve.wait_ge(l_o.s, l_o.at(l, 1))
                V.tensor_tensor(tmp[RR, 4, :], PS[RR, 4, 0:T], sinm[RR, :], ALU.mult).then_inc(kt_t.s, 1)
                V.tensor_tensor(kr[RR, :], kr[RR, :], cosm[RR, :], ALU.mult).then_inc(kt_c.s, 1)
                dve.wait_ge(kt_t.s, kt_t.at(l, 1))
                dve.wait_ge(kt_c.s, kt_c.at(l, 1))
                for half in range(2):
                    V.tensor_tensor(CD[RR, 4 * half:4 * half + 4, :], kr[RR, :].unsqueeze(1).to_broadcast([32, 4, T]),
                                    tmp[RR, 4, :].unsqueeze(1).to_broadcast([32, 4, T]), ALU.add).then_inc(kt.s, 1)
                for i in range(4):
                    if i % 2 == 0:
                        split_block(l, 18 + i // 2)
                    dve.wait_ge(qt_ps.s, qt_ps.at(l, i + 1))
                    two = tmp[RR, 2 * (i % 2):2 * (i % 2) + 2, :]
                    q2 = AB[RR, 2 * i:2 * i + 2, :]
                    c2, s2 = (t[RR, :].unsqueeze(1).to_broadcast([32, 2, T]) for t in (cosm, sinm))
                    V.tensor_tensor(two, PS[RR, (3, 5)[i % 2], :].rearrange("p (a b) -> p a b", a=2), s2, ALU.mult).then_inc(qt_t.s, 1)
                    V.tensor_tensor(q2, q2, c2, ALU.mult).then_inc(qt_c.s, 1)
                    dve.wait_ge(qt_t.s, qt_t.at(l, i + 1))
                    dve.wait_ge(qt_c.s, qt_c.at(l, i + 1))
                    V.tensor_tensor(q2, q2, two, ALU.add).then_inc(qt.s, 1)
                split_block(l, 20)
                dve.wait_ge(l_ohi.s, l_ohi.at(l, 1))
                V.tensor_tensor(ob_lo[:, 0:4, :], EF[:, 4:8, :], ob_hi[:, 0:4, :].bitcast(F32), ALU.subtract).then_inc(l_olo.s, 1)

                def softmax_scores(h):
                    b = (3, 5)[h % 2]
                    pb = pbuf[:, h % 2, :]
                    m = mx[:, h % 2, :]
                    dve.wait_ge(s_ps.s, s_ps.at(l, h + 1))
                    if h >= 2:
                        dve.wait_ge(s_tp.s, s_tp.at(l, h - 1))
                    V.scalar_tensor_tensor(pb, PS[:, b, 0:384], SCALE, mask, ALU.mult, ALU.add).then_inc(s_m.s, 1)
                    dve.wait_ge(s_m.s, s_m.at(l, h + 1))
                    V.tensor_reduce(m[:, 0:1], pb[:, 0:P], AX_X, ALU.max)
                    V.tensor_reduce(m[:, 1:2], pb[:, P:3 * P], AX_X, ALU.max).then_inc(s_max.s, 1)
                    dve.wait_ge(s_max.s, s_max.at(l, h + 1))
                    V.tensor_scalar(m[:, 2:4], m[:, 0:2], -1.0, None, ALU.mult).then_inc(s_neg.s, 1)

                def softmax_norm(h):
                    pb = pbuf[:, h % 2, :]
                    m = mx[:, h % 2, :]
                    dve.wait_ge(s_e.s, s_e.at(l, h + 1))
                    V.reciprocal(m[:, 6:8], m[:, 4:6]).then_inc(s_rc.s, 1)
                    dve.wait_ge(s_rc.s, s_rc.at(l, h + 1))
                    V.tensor_scalar(pb[:, 0:P], pb[:, 0:P], m[:, 6:7], None, ALU.mult)
                    V.tensor_scalar(pb[:, P:3 * P], pb[:, P:3 * P], m[:, 7:8], None, ALU.mult).then_inc(s_n.s, 1)

                def merge(m):
                    b, i = m // 4, m % 4
                    y = PS[:, 0, :]
                    if m % 2 == 0:
                        dve.wait_ge(my_ps.s, my_ps.at(l, m // 2 + 1))
                    else:
                        product_done(dve, l, J[("gate", b, i)])
                    dve.wait_ge(mg_th.s, mg_th.at(l, m + 1))
                    if b == 0:
                        V.scalar_tensor_tensor(flat2(h32, i), flat2(lat, m % 2), 1.0, y, ALU.add, ALU.mult).then_inc(mg_y.s, 1)
                        dve.wait_ge(mg_y.s, mg_y.at(l, m + 1))
                        dve.sem_inc(m_acc.s, 1)
                        return
                    t = flat2(EF, 2 + m % 2)
                    V.scalar_tensor_tensor(t, flat2(lat, m % 2), 1.0, y, ALU.add, ALU.mult).then_inc(mg_y.s, 1)
                    dve.wait_ge(mg_y.s, mg_y.at(l, m + 1))
                    V.tensor_tensor(flat2(h32, i), flat2(h32, i), t, ALU.add).then_inc(m_acc.s, 1)

                def merged_lo(i):
                    dve.wait_ge(m_hi.s, m_hi.at(l, i + 1))
                    hi, lo = (ob_hi, ob_lo) if i < 2 else (oa_hi, oa_lo)
                    V.scalar_tensor_tensor(flat2(lo, i % 2), flat2(h32, i), 0.5, flat2(hi, i % 2).bitcast(F32), ALU.mult,
                                           ALU.subtract).then_inc(m_lo.s, 1)

                softmax_scores(0)
                for m in range(12):
                    j = J[("gate", 0, 0)] + 3 * (m // 2)
                    if m < HEADS:
                        softmax_norm(m)
                    if m < HEADS - 1:
                        softmax_scores(m + 1)
                    if m % 2 == 0:
                        split_block(l, j + RING)
                    merge(m)
                    if m % 2 == 1:
                        split_block(l, j + RING + 1)
                        split_block(l, j + RING + 2)
                    if m in (3, 7):
                        i = m // 4
                        dve.wait_ge(m_ohi.s, m_ohi.at(l, i + 1))
                        V.tensor_tensor(flat2(oa_lo, i), PS[:, 2, :], flat2(oa_hi, i).bitcast(F32), ALU.subtract).then_inc(m_olo.s, 1)
                    if m in (8, 9):
                        merged_lo(m - 8)
                merged_lo(2)
                merged_lo(3)
                for j in range(39, NM):
                    split_block(l, j)
                half_end(l, 0)

                half_start(l, 1, NM)

                def conv(n, part, i):
                    dve.wait_ge(up_c0.s, up_c0.at(l, n + 1))
                    for tap in (1, 0):
                        d = 2 - tap
                        for b in range(2):
                            v = V.scalar_tensor_tensor(
                                EF[:, 2 * part + b, d:T], PS[:, 4 + part, T * b:T * b + T - d],
                                cur[:, bass.ds(i * 2 + col[f"tap{tap}"] + NFF * part + b, 1)],
                                EF[:, 2 * part + b, d:T], ALU.mult, ALU.add)
                        if tap == 1:
                            v.then_inc(up_c1.s, 1)
                            dve.wait_ge(up_c1.s, up_c1.at(l, n + 1))
                        else:
                            v.then_inc(up_c.s, 1)

                def hidden(i):
                    dve.wait_ge(f_gl.s, f_gl.at(l, i + 1))
                    V.tensor_tensor(flat2(tmp, 0), flat2(EF, 1), flat2(EF, 0), ALU.mult).then_inc(f_t.s, 1)

                def hidden_lo(i):
                    dve.wait_ge(f_hi.s, f_hi.at(l, i + 1))
                    V.tensor_tensor(flat2(oa_lo, 0), flat2(tmp, 0), flat2(oa_hi, 0).bitcast(F32), ALU.subtract).then_inc(f_lo.s, 1)

                def ffn_split(i, part):
                    slot = (NM + 2 + part) % RING
                    dve.wait_ge(hi_ready.s, hi_ready.at(l, i * 3 + (NM + 3 + part)))
                    V.tensor_tensor(w_lo[:, slot, :], raw[:, slot, :], w_hi[:, slot, :].bitcast(F32), ALU.subtract).then_inc(lo_ready.s, 1)

                conv(0, 0, 0)
                split_block(l, NM + 3)
                conv(1, 1, 0)
                split_block(l, NM + 4)
                hidden(0)
                hidden_lo(0)
                with dve.Fori(1, PAIRS - 1) as i:
                    conv(i * 2, 0, i)
                    ffn_split(i, 0)
                    conv(i * 2 + 1, 1, i)
                    ffn_split(i, 1)
                    hidden(i)
                    ffn_split(i, 2)
                    hidden_lo(i)
                i = PAIRS - 1
                conv(i * 2, 0, i)
                ffn_split(i, 0)
                conv(i * 2 + 1, 1, i)
                hidden(i)
                hidden_lo(i)
                half_end(l, 1)

        @blk.tensor
        def _(pe):
            MM = nc.tensor.matmul

            def mm3(ps, w_pair, a_pair, first, last, weights_move=False):
                (wh, wl), (ah, al) = w_pair, a_pair
                for n, (w, a) in enumerate(((wh, al), (wl, ah), (wh, ah))):
                    lhs, rhs = (a, w) if weights_move else (w, a)
                    ins = MM(ps, lhs, rhs, start=first and n == 0, stop=last and n == 2)
                return ins

            pe.wait_ge(rows_in, 16 * sum(len(v) for v in layout))
            pe.wait_ge(cst_in, 16)
            rowbuf = tmp[:].rearrange("p a b -> p (a b)")[:, 0:L * 3 * P].rearrange("p (l c n) -> p l c n", l=L, c=3)
            for n in range(3 * L):
                u = used[n % 3]
                nc.tensor.transpose(PS[:, n, 0:u], rowbuf[0:u, n // 3, n % 3, :], ident[0:u, 0:u]).then_inc(par_ps, 1)
            for g in range(G0):
                pe.wait_ge(ada0_done, g + 1)
                for b in range(2):
                    ins = MM(PS[:, ADA_BANK, 2 * g + b:2 * g + b + 1], h32[:, g, P * b:P * b + P], ones[:, 0:1],
                             start=True, stop=True)
            ins.then_inc(ada0_sum, 1)

            def ada_part(n, g):
                slot = g % 2 if isinstance(g, int) else None
                pe.wait_ge(acc_ready, n + 1)
                for b in range(2):
                    ins = MM(PS[:, ADA_BANK, 2 * g + b:2 * g + b + 1], adacc[:, slot, P * b:P * b + P], ones[:, 0:1],
                             start=True, stop=True)
                ins.then_inc(ada_sum, 1)

            for g in range(G0, GROUPS):
                ada_part(g - G0, g)

            def flat2(t, i):
                return t[:, 2 * i:2 * i + 2, :].rearrange("p a b -> p (a b)")

            def half_start(l, ph):
                for c in range(TC):
                    n = 2 * ph + c
                    src = (AB, CD)[c][:].rearrange("p a b -> p (a b)")[:, D:2 * D]
                    pe.wait_ge(n_xn.s, n_xn.at(l, n + 1))
                    if c == 0 and ph == 0:
                        pe.wait_ge(par_ready, 3 * L)
                    for half in range(2):
                        bank = (4, 0)[c] + half
                        for k in range(4):
                            kk = 4 * half + k
                            ins = nc.tensor.transpose(PS[:, bank, P * k:P * k + P], src[:, P * kk:P * kk + P], ident)
                        ins.then_inc(n_tp.s, 1)
                pe.wait_ge(mod_ready.s, mod_ready.at(l, 2 * ph + 2))
                for i in range(2):
                    for k in range(4):
                        g = gcol[:, 4 * i + k:4 * i + k + 1].to_broadcast([P, P])
                        ins = MM(PS[:, (6, 3)[i], P * k:P * k + P], g, ident, start=True, stop=True)
                    ins.then_inc(grow_ps.s, 1)
                pe.wait_ge(n_lo.s, n_lo.at(l, 2 * ph + 2))

            def weights(j):
                return block_shape(w_hi, j), block_shape(w_lo, j)

            def ready(l, j):
                pe.wait_ge(lo_ready.s, lo_ready.at(l, RING + j + 1))

            def h_pair(k, cs=slice(0, T)):
                return h_hi[:, k, cs], h_lo[:, k, cs]

            def two_tiles(l, j, bank):
                ready(l, j)
                if j == J[("c", 2)]:
                    wh, wl = (t[:, j % RING, :].rearrange("p (k n) -> p k n", k=DK) for t in (w_hi, w_lo))
                else:
                    wh, wl = weights(j)
                for b in range(2):
                    for k in range(DK):
                        ins = mm3(PS[:, bank, T * b:T * b + T],
                                  (wh[:, k, P * b:P * b + P], wl[:, k, P * b:P * b + P]), h_pair(k), k == 0, k == DK - 1)
                ins.then_inc(blk_used.s, 1)

            with pe.Fori(0, L) as l:
                ada_n = l * 2 * GROUPS + (GROUPS - G0)
                half_start(l, 0)
                for j in range(4):
                    two_tiles(l, j, (2, 4, 5, 0)[j])
                ada_part(ada_n, 0)
                pe.wait_ge(grow_ev.s, grow_ev.at(l, 2))
                for i in range(2):
                    j = 4 + i
                    ready(l, j)
                    wh, wl = weights(j)
                    for c in range(TC):
                        for k in range(4):
                            kk = 4 * i + k
                            ins = mm3(PS[:, (1, 3)[c], :], (wh[:, k, :], wl[:, k, :]), h_pair(kk, slice(P * c, P * c + P)),
                                      kk == 0, kk == DK - 1, weights_move=True)
                    ins.then_inc(blk_used.s, 1)
                ada_part(ada_n + 1, 1)
                def rotate(i):
                    pe.wait_ge(qk_ev.s, qk_ev.at(l, i + 1))
                    MM(PS[:, (6, 2, 5, 0)[i], :], rot_r, flat2(AB, i), start=True, stop=True).then_inc(rot_ps.s, 1)

                rotate(0)
                rotate(1)
                two_tiles(l, 6, 4)
                rotate(2)
                rotate(3)
                pe.wait_ge(v_ev.s, v_ev.at(l, 2))
                two_tiles(l, 7, 1)
                ada_part(ada_n + 2, 2)
                pe.wait_ge(rot_t.s, rot_t.at(l, 2))
                two_tiles(l, 8, 3)
                two_tiles(l, 9, 6)

                def ret_score(h):
                    r = slice(64 * (h % 2), 64 * (h % 2) + 64)
                    q, k = AB[r, h // 2, :], AB[r, 4 + h // 2, :]
                    bank = (2, 4)[h % 2]
                    if h >= 2:
                        pe.wait_ge(rs_p.s, rs_p.at(l, h - 1))
                    MM(PS[:, bank, 0:T], k[:, 0:P], q, start=True, stop=True)
                    MM(PS[:, bank, T:T + P], k[:, P:T], q[:, P:T], start=True, stop=True).then_inc(rs_ps.s, 1)

                def ret_av(h):
                    pe.wait_ge(rs_p.s, rs_p.at(l, h + 1))
                    r = slice(64 * (h % 2), 64 * (h % 2) + 64)
                    y = PS[r, (3, 5)[h // 4], T * (h // 2 % 2):T * (h // 2 % 2) + T]
                    pb = pbuf[:, h % 2, :]
                    v = CD[:, 0:4, :].rearrange("p (c a) b -> p c (a b)", c=2)
                    MM(y, v[:, 0, 64 * h:64 * h + 64], pb[:, 0:T], start=True, stop=False)
                    MM(y[:, P:T], v[:, 1, 64 * h:64 * h + 64], pb[:, T:T + P], start=False, stop=True).then_inc(rs_av.s, 1)

                pe.wait_ge(rot_t.s, rot_t.at(l, 4))
                pe.wait_ge(g_ev.s, g_ev.at(l, 2))
                two_tiles(l, 10, 2)
                ada_part(ada_n + 3, 3)
                two_tiles(l, 11, 4)
                pe.wait_ge(rope.s, rope.at(l, 4))
                pe.wait_ge(lx_c.s, lx_c.at(l, 12))
                two_tiles(l, 12, 5)
                pe.wait_ge(lg_ev.s, lg_ev.at(l, 2))
                ret_score(0)
                ret_score(1)
                two_tiles(l, 13, 0)
                ret_av(0)
                ret_av(1)
                ret_score(2)
                ret_score(3)
                two_tiles(l, 14, 1)
                ada_part(ada_n + 4, 4)
                ret_av(2)
                ret_av(3)
                ret_score(4)
                ret_score(5)
                pe.wait_ge(c_sq.s, c_sq.at(l, 1))
                ret_av(4)
                ret_av(5)
                ret_score(6)
                ret_score(7)
                ret_av(6)
                ret_av(7)
                pe.wait_ge(rs_p.s, rs_p.at(l, 8))
                for i in range(5):
                    part = 0 if i < QK else 1
                    ins = MM(PS[:, 2, T * part:T * part + T], ones, tmp[:, i, :], start=i in (0, QK), stop=i in (QK - 1, 4))
                ins.then_inc(cs_ps.s, 1)
                pe.wait_ge(kr_ev.s, kr_ev.at(l, 1))
                for i in range(2):
                    pe.wait_ge(ry_ev.s, ry_ev.at(l, i + 1))
                    MM(PS[:, (0, 1)[i], :], center, flat2(AB, i), start=True, stop=True).then_inc(ry_ps.s, 1)
                pe.wait_ge(wbd_in.s, wbd_in.at(l, 256))

                def lru_gate(i):
                    for b in range(2):
                        t = 2 * (i % 2) + b
                        ins = MM(PS[:, (5, 6, 4, 0)[i], T * b:T * b + T], wbd[:, i // 2, t, :], EF[:, t, :], start=True, stop=True)
                    ins.then_inc(lr_ps.s, 1)

                lru_gate(0)
                lru_gate(1)
                lru_gate(2)
                for i in range(2):
                    pe.wait_ge(rv_sq.s, rv_sq.at(l, i + 1))
                    if i == 0:
                        pe.wait_ge(cs_sd.s, cs_sd.at(l, 1))
                    MM(PS[:, (2, 3)[i], :], mean64, flat2(tmp, i), start=True, stop=True).then_inc(rv_ps.s, 1)
                pe.wait_ge(r_yn.s, r_yn.at(l, 2))
                lru_gate(3)
                pe.wait_ge(cn_lo.s, cn_lo.at(l, 1))
                pe.wait_ge(rv_sd.s, rv_sd.at(l, 2))
                for i in range(2):
                    j = 15 + i
                    ready(l, j)
                    wh, wl = weights(j)
                    for pair in range(2):
                        bank = (2, 3, 5, 6)[2 * i + pair]
                        if i == 1 and pair == 0:
                            pe.wait_ge(lr_ev.s, lr_ev.at(l, 1))
                        for b in range(2):
                            cols = slice(DQK * (2 * pair + b), DQK * (2 * pair + b) + DQK)
                            for k in range(QK):
                                ins = mm3(PS[0:DQK, bank, T * b:T * b + T], (wh[:, k, cols], wl[:, k, cols]),
                                          (ob_hi[:, k, :], ob_lo[:, k, :]), k == 0, k == QK - 1)
                        ins.then_inc(uq_ps.s if pair == 0 else blk_used.s, 1)
                ready(l, 17)
                wh, wl = (t[:, 17 % RING, :].rearrange("p (k two n) -> p k two n", k=KVK, two=2) for t in (w_hi, w_lo))
                pe.wait_ge(lr_ev.s, lr_ev.at(l, 2))
                for i in range(2):
                    for b in range(2):
                        t = 2 * i + b
                        for k in range(KVK):
                            ins = mm3(PS[:, (4, 0)[i], T * b:T * b + T], (wh[:, k, 0, P * t:P * t + P], wl[:, k, 0, P * t:P * t + P]),
                                      (ob_hi[:, QK + k, :], ob_lo[:, QK + k, :]), k == 0, k == KVK - 1)
                    ins.then_inc(uk_ps.s, 1)
                pe.wait_ge(uq_ev.s, uq_ev.at(l, 1))
                for c in range(TC):
                    for k in range(KVK):
                        cs = slice(P * c, P * c + P)
                        ins = mm3(PS[:, (1, 2)[c], :], (wh[:, k, 1, :], wl[:, k, 1, :]),
                                  (ob_hi[:, QK + k, cs], ob_lo[:, QK + k, cs]), k == 0, k == KVK - 1, weights_move=True)
                    ins.then_inc(uv_ps.s if c == 0 else blk_used.s, 1)
                ada_part(ada_n + 5, 5)
                pe.wait_ge(uk_ev.s, uk_ev.at(l, 1))
                MM(PS[:, 4, 0:T], rot_m, kr[:], start=True, stop=True).then_inc(kt_ps.s, 1)
                for i in range(4):
                    if i == 0:
                        pe.wait_ge(uq_ev.s, uq_ev.at(l, 4))
                    if i >= 2:
                        pe.wait_ge(qt_t.s, qt_t.at(l, i - 1))
                    MM(PS[0:DQK, (3, 5)[i % 2], :], rot_m[0:DQK, 0:DQK],
                       AB[0:DQK, 2 * i:2 * i + 2, :].rearrange("p a b -> p (a b)"), start=True, stop=True).then_inc(qt_ps.s, 1)

                def mla_score(h):
                    bank = (3, 5)[h % 2]
                    q, k = AB[0:DQK, h, :], CD[0:DQK, h, :]
                    if h >= 2:
                        pe.wait_ge(s_m.s, s_m.at(l, h - 1))
                    MM(PS[:, bank, 0:P], q[:, 0:P], k[:, 0:P], start=True, stop=True)
                    MM(PS[:, bank, P:3 * P], q[:, P:T], k, start=True, stop=True).then_inc(s_ps.s, 1)

                def mla_transpose(h):
                    pb = pbuf[:, h % 2, :]
                    pe.wait_ge(s_n.s, s_n.at(l, h + 1))
                    if h >= 1:
                        pe.wait_ge(s_tev.s, s_tev.at(l, h))
                    for i in range(3):
                        ins = nc.tensor.transpose(PS[:, 1, P * i:P * i + P], pb[:, P * i:P * i + P], ident)
                    ins.then_inc(s_tp.s, 1)

                def mla_av(h):
                    pe.wait_ge(s_tev.s, s_tev.at(l, h + 1))
                    r = slice(64 * (h % 2), 64 * (h % 2) + 64)
                    o = PS[r, 2, T * (h // 2 % 2):T * (h // 2 % 2) + T]
                    if h == 4:
                        pe.wait_ge(m_olo.s, m_olo.at(l, 1))
                    v = EF[:, 0:4, :].rearrange("p (c a) b -> p c (a b)", c=2)
                    pt = ptb[:, h % 2, :]
                    MM(o, v[:, 0, 64 * h:64 * h + 64], pt[:, 0:T], start=True, stop=False)
                    MM(o[:, P:T], v[:, 1, 64 * h:64 * h + 64], pt[:, T:T + P], start=False, stop=True).then_inc(s_av.s, 1)

                def merge_y(b, i, wj):
                    m = 4 * b + i
                    if m >= 1:
                        pe.wait_ge(mg_y.s, mg_y.at(l, m))
                    wh, wl = weights(wj)
                    oh, ol = ((oa_hi, oa_lo), (ob_hi, ob_lo), (oa_hi, oa_lo))[b]
                    for t in range(2):
                        cols = slice(P * (2 * (i % 2) + t), P * (2 * (i % 2) + t) + P)
                        for k in range(WK):
                            ins = mm3(PS[:, 0, T * t:T * t + T], (wh[:, k, cols], wl[:, k, cols]), (oh[:, k, :], ol[:, k, :]),
                                      k == 0, k == WK - 1)
                    return ins

                pe.wait_ge(qt.s, qt.at(l, 1))
                pe.wait_ge(kt.s, kt.at(l, 2))
                pe.wait_ge(uk_ev.s, uk_ev.at(l, 2))
                pe.wait_ge(uv_ev.s, uv_ev.at(l, 2))
                pe.wait_ge(qt.s, qt.at(l, 4))
                pe.wait_ge(kt_t.s, kt_t.at(l, 1))
                mla_score(0)
                for m in range(12):
                    b, i = m // 4, m % 4
                    gj, wj = J[("gate", b, i)], J[("wo", b, i // 2)]
                    if m < HEADS - 1:
                        mla_score(m + 1)
                    ready(l, gj)
                    if m >= 2:
                        pe.wait_ge(mg_th.s, mg_th.at(l, m - 1))
                    wh, wl = weights(gj)
                    for t in range(2):
                        for k in range(DK):
                            ins = mm3(PS[:, (4, 6)[m % 2], T * t:T * t + T],
                                      (wh[:, k, P * t:P * t + P], wl[:, k, P * t:P * t + P]), h_pair(k), k == 0, k == DK - 1)
                    ins.then_inc(blk_used.s if m % 2 == 0 else mg_ps.s, 1)
                    if m < HEADS:
                        mla_transpose(m)
                    if i == 0:
                        sg, n = ((r_olo, 2), (l_olo, 1), (m_olo, 2))[b]
                        pe.wait_ge(sg.s, sg.at(l, n))
                    if i % 2 == 0:
                        ready(l, wj)
                    ins = merge_y(b, i, wj)
                    if i % 2 == 0:
                        ins.then_inc(my_ps.s, 1)
                    else:
                        ins.then_inc(blk_used.s, 2)
                    if m < HEADS:
                        mla_av(m)
                    if m % 2 == 1:
                        ada_part(ada_n + 6 + m // 2, 6 + m // 2)

                pe.wait_ge(m_acc.s, m_acc.at(l, 12))
                for i in range(4):
                    j = 36 + i
                    hi, lo = (ob_hi, ob_lo) if i < 2 else (oa_hi, oa_lo)
                    pe.wait_ge(m_lo.s, m_lo.at(l, i + 1))
                    ready(l, j)
                    wh, wl = weights(j)
                    for c in range(TC):
                        cs = slice(P * c, P * c + P)
                        for half in range(2):
                            ns = slice(512 * half, 512 * half + 512)
                            for k in range(2):
                                kk = 2 * (i % 2) + k
                                ins = mm3(PS[:, 2 * c + half, :], (wh[:, k, ns], wl[:, k, ns]), (hi[:, kk, cs], lo[:, kk, cs]),
                                          i == 0 and k == 0, i == 3 and k == 1, weights_move=True)
                        if c == 1:
                            ins.then_inc(blk_used.s, 1)
                        elif i == 3:
                            ins.then_inc(y_ps.s, 1)

                half_start(l, 1)
                ffn_n = ada_n + GROUPS

                def up_proj(n, part, slot, j_done):
                    pe.wait_ge(lo_ready.s, lo_ready.at(l, j_done))
                    wh, wl = ffn_shape(w_hi, slot, "up"), ffn_shape(w_lo, slot, "up")
                    for b in range(2):
                        for k in range(DK):
                            ins = mm3(PS[:, 4 + part, T * b:T * b + T],
                                      (wh[:, k, P * b:P * b + P], wl[:, k, P * b:P * b + P]), h_pair(k), k == 0, k == DK - 1)
                    ins.then_inc(blk_used.s, 1)

                def down_proj(i, slot, j_done, first, last):
                    pe.wait_ge(lo_ready.s, lo_ready.at(l, j_done))
                    pe.wait_ge(f_lo.s, f_lo.at(l, i + 1))
                    wh, wl = ffn_shape(w_hi, slot, "down"), ffn_shape(w_lo, slot, "down")
                    for c in range(TC):
                        cs = slice(P * c, P * c + P)
                        for half in range(2):
                            ns = slice(512 * half, 512 * half + 512)
                            for k in range(2):
                                ins = mm3(PS[:, 2 * c + half, :], (wh[:, k, ns], wl[:, k, ns]), (oa_hi[:, k, cs], oa_lo[:, k, cs]),
                                          first and k == 0, last and k == 1, weights_move=True)
                        if c == 1:
                            ins.then_inc(blk_used.s, 1)
                        elif last:
                            ins.then_inc(y_ps.s, 1)

                s_u, s_g, s_d = (NM + 2) % RING, NM % RING, (NM + 1) % RING
                up_proj(0, 0, NM % RING, RING + NM + 1)
                ada_part(ffn_n, 0)
                up_proj(1, 1, (NM + 1) % RING, RING + NM + 2)

                def pair(i, ada_g, first):
                    pe.wait_ge(up_c.s, up_c.at(l, i * 2 - 1))
                    up_proj(i * 2, 0, s_u, i * 3 + (RING + NM))
                    pe.wait_ge(up_c.s, up_c.at(l, i * 2))
                    up_proj(i * 2 + 1, 1, s_g, i * 3 + (RING + NM + 1))
                    if first:
                        pe.wait_ge(grow_ev.s, grow_ev.at(l, 4))
                    down_proj(i - 1, s_d, i * 3 + (RING + NM + 2), first, False)
                    if ada_g is not None:
                        ada_part(i + ffn_n, ada_g)

                pair(1, 1, True)
                with pe.Fori(1, PAIRS // 2) as it:
                    for b in range(2):
                        i = it * 2 + b
                        pair(i, None, False)
                        pe.wait_ge(acc_ready, i + ffn_n + 1)
                        for c in range(2):
                            ins = MM(PS[:, ADA_BANK, bass.ds(i * 2 + c, 1)], adacc[:, b, P * c:P * c + P], ones[:, 0:1],
                                     start=True, stop=True)
                        ins.then_inc(ada_sum, 1)
                pair(PAIRS - 1, PAIRS - 1, False)
                ada_part(ffn_n + PAIRS, PAIRS)
                down_proj(PAIRS - 1, s_u, RING + NB, False, True)

    return nc


_INS = ["x", "c", "positions", "ada_w", "ada_b", "mix_pre_g", "mix_post_g", "w_in", "lru_conv_w", "lru_conv_b", "lru_wa",
        "lru_ba", "lru_wx", "lru_bx", "lru_lambda", "lru_wo", "ret_wo", "mla_q_norm_g", "mla_w_uq", "mla_kv_norm_g",
        "mla_w_ukv", "mla_wo", "w_out", "ffn_pre_g", "ffn_post_g", "ffn_w_up", "ffn_conv_w", "ffn_conv_b", "ffn_w_down"]


def kernel(**inputs):
    import concourse.bacc as bacc
    from concourse.bass_utils import run_bass_kernel_spmd as run

    nc = bacc.Bacc("TRN2", target_bir_lowering=False, num_devices=1)
    arrays, aps = {}, {}
    for name in _INS:
        a = np.ascontiguousarray(inputs[name])
        arrays[f"in_{name}"] = a
        aps[name] = nc.dram_tensor(f"in_{name}", a.shape, mybir.dt.from_np(a.dtype), kind="ExternalInput").ap()
    shape = tuple(inputs["x"].shape)
    table = constants(shape[1])
    arrays["shape_constants"] = table
    consts = nc.dram_tensor("shape_constants", table.shape, F32, kind="ExternalInput").ap()
    out = nc.dram_tensor("out", shape, F32, kind="ExternalOutput").ap()
    trunk_kernel(nc, aps, consts, out)
    r = run(nc, [arrays], core_ids=[0])
    return r.results[0]["out"]
```
